# Optimizing a Trainium2 kernel written in Bass

```python
import jax, jax.numpy as jnp
from jax import lax
import numpy as np
import jax
import jax.numpy as jnp

D_MODEL = 1024
BATCH = 1
SEQ = 256
DEPTH = 2

MLA_HEADS = 8
QK_NOPE_DIM = 64
QK_ROPE_DIM = 32
QK_HEAD_DIM = QK_NOPE_DIM + QK_ROPE_DIM
V_HEAD_DIM = 64
Q_LORA_RANK = 384
KV_LORA_RANK = 256
ROPE_THETA = 10000.0
Q_BLOCK = 128
RWKV_HEAD_DIM = 64
RWKV_HEADS = 4
RWKV_WIDTH = RWKV_HEADS * RWKV_HEAD_DIM
DECAY_LORA = 64
AAA_LORA = 64
GATE_LORA = 128
MV_LORA = 32
GN_EPS = 64e-5
CONV_WIDTH = 256
CONV_K = 3
D_FF = 4 * D_MODEL
N_BRANCH = 3
NORM_EPS = 1e-6

GATE_COLS = N_BRANCH * D_MODEL
MLA_COLS = Q_LORA_RANK + KV_LORA_RANK + QK_ROPE_DIM
RWKV_COLS = 3 * RWKV_WIDTH + DECAY_LORA + AAA_LORA + GATE_LORA
CONV_COLS = 3 * CONV_WIDTH
IN_COLS = GATE_COLS + MLA_COLS + RWKV_COLS + CONV_COLS


def _split(x, sizes):
    idx = np.cumsum(sizes)[:-1].tolist()
    return jnp.split(x, idx, axis=-1)

def rms_norm(x, g, eps=NORM_EPS):
    xf = x.astype(jnp.float32)
    y = xf * lax.rsqrt(jnp.mean(xf * xf, axis=-1, keepdims=True) + eps)
    return (y * g.astype(jnp.float32)).astype(x.dtype)

def token_shift(x):
    return jnp.pad(x, ((0, 0), (1, 0), (0, 0)))[:, :-1]

def rope_tables(positions):
    freqs = ROPE_THETA ** (-(jnp.arange(QK_ROPE_DIM // 2, dtype=jnp.float32) * 2.0 / QK_ROPE_DIM))
    ang = positions.astype(jnp.float32)[..., None] * freqs
    return jnp.cos(ang)[:, :, None, :], jnp.sin(ang)[:, :, None, :]

def apply_rope(x, cos, sin):
    x1, x2 = x[..., :QK_ROPE_DIM // 2], x[..., QK_ROPE_DIM // 2:]
    cos, sin = cos.astype(x.dtype), sin.astype(x.dtype)
    return jnp.concatenate([x1 * cos - x2 * sin, x1 * sin + x2 * cos], axis=-1)

def causal_block_attention(q, k, v):
    scale = QK_HEAD_DIM ** -0.5
    qh, kh, vh = (jnp.swapaxes(t, 1, 2) for t in (q, k, v))
    seq = qh.shape[2]
    outs = []
    for start in range(0, seq, Q_BLOCK):
        stop = start + Q_BLOCK
        s = jnp.einsum('bhqd,bhkd->bhqk', qh[:, :, start:stop], kh[:, :, :stop]).astype(jnp.float32) * scale
        causal = (start + jnp.arange(Q_BLOCK))[:, None] >= jnp.arange(stop)[None, :]
        p = jax.nn.softmax(jnp.where(causal, s, -jnp.inf), axis=-1)
        outs.append(jnp.einsum('bhqk,bhkd->bhqd', p.astype(vh.dtype), vh[:, :, :stop]))
    return jnp.swapaxes(jnp.concatenate(outs, axis=2), 1, 2)

def mla_branch(cols, positions, q_a_norm, wq_b, kv_a_norm, wkv_b, q_norm, k_norm):
    bsz, seq, _ = cols.shape
    c_q, c_kv, k_pe = _split(cols, [Q_LORA_RANK, KV_LORA_RANK, QK_ROPE_DIM])
    q = (rms_norm(c_q, q_a_norm) @ wq_b).reshape(bsz, seq, MLA_HEADS, QK_HEAD_DIM)
    kv = (rms_norm(c_kv, kv_a_norm) @ wkv_b).reshape(bsz, seq, MLA_HEADS, QK_NOPE_DIM + V_HEAD_DIM)
    k_nope, v = kv[..., :QK_NOPE_DIM], kv[..., QK_NOPE_DIM:]
    k_pe = jnp.broadcast_to(k_pe[:, :, None, :], (bsz, seq, MLA_HEADS, QK_ROPE_DIM))
    k = jnp.concatenate([k_nope, k_pe], axis=-1)
    q = rms_norm(q, q_norm)
    k = rms_norm(k, k_norm)
    cos, sin = rope_tables(positions)
    q = jnp.concatenate([q[..., :QK_NOPE_DIM], apply_rope(q[..., QK_NOPE_DIM:], cos, sin)], axis=-1)
    k = jnp.concatenate([k[..., :QK_NOPE_DIM], apply_rope(k[..., QK_NOPE_DIM:], cos, sin)], axis=-1)
    o = causal_block_attention(q, k, v)
    return o.reshape(bsz, seq, MLA_HEADS * V_HEAD_DIM)

def wkv7_scan(r, w, k, v, a, b):
    def step(state, inp):
        r_t, w_t, k_t, v_t, a_t, b_t = inp
        sa = jnp.einsum('bhvk,bhk->bhv', state, a_t)
        state = state * w_t[:, :, None, :] + sa[..., None] * b_t[:, :, None, :] + v_t[..., None] * k_t[:, :, None, :]
        return state, jnp.einsum('bhvk,bhk->bhv', state, r_t)
    bsz, _, heads, n = r.shape
    xs = tuple(jnp.moveaxis(t, 1, 0) for t in (r, w, k, v, a, b))
    s0 = jnp.zeros((bsz, heads, n, n), jnp.float32)
    _, ys = lax.scan(step, s0, xs)
    return jnp.moveaxis(ys, 0, 1)

def rwkv7_branch(cols, h, v_first, mu, w0, w2, a0, a2, g2, k_k, k_a, r_k, ln_w, ln_b, vres):
    bsz, seq, _ = cols.shape
    f32 = jnp.float32
    cols = cols + (token_shift(cols) - cols) * mu
    r, k, v, xw, xa, xg = _split(cols, [RWKV_WIDTH, RWKV_WIDTH, RWKV_WIDTH, DECAY_LORA, AAA_LORA, GATE_LORA])
    log_w = -jax.nn.softplus(-(w0 + jnp.tanh(xw) @ w2).astype(f32)) - 0.5
    decay = jnp.exp(-jnp.exp(log_w))
    a = jax.nn.sigmoid(a0 + xa @ a2)
    g = jax.nn.sigmoid(xg) @ g2
    if vres is None:
        v_first = v
    else:
        v1, v_mu, v0, v2 = vres
        xv = h @ v1
        xv = xv + (token_shift(xv) - xv) * v_mu
        v = v + (v_first - v) * jax.nn.sigmoid(v0 + xv @ v2)
    heads = lambda t: t.reshape(bsz, seq, RWKV_HEADS, RWKV_HEAD_DIM).astype(f32)
    kk = heads(k * k_k)
    kk = kk / jnp.maximum(jnp.linalg.norm(kk, axis=-1, keepdims=True), 1e-12)
    k = k * (1 + (a - 1) * k_a)
    rh, kh, vh, ah = heads(r), heads(k), heads(v), heads(a)
    y = wkv7_scan(rh, heads(decay), kh, vh, -kk, kk * ah)
    mean = jnp.mean(y, axis=-1, keepdims=True)
    var = jnp.mean(jnp.square(y - mean), axis=-1, keepdims=True)
    y = ((y - mean) * lax.rsqrt(var + GN_EPS)).reshape(bsz, seq, RWKV_WIDTH)
    y = y * ln_w.astype(f32) + ln_b.astype(f32)
    bonus = jnp.sum(rh * kh * r_k.astype(f32), axis=-1, keepdims=True) * vh
    y = (y + bonus.reshape(bsz, seq, RWKV_WIDTH)).astype(cols.dtype)
    return y * g, v_first

def short_conv_branch(cols, conv_w):
    b_gate, c_gate, xc = _split(cols, [CONV_WIDTH, CONV_WIDTH, CONV_WIDTH])
    u = c_gate * xc
    y = lax.conv_general_dilated(
        u, conv_w.astype(u.dtype)[:, None, :], window_strides=(1,), padding=[(CONV_K - 1, 0)],
        dimension_numbers=('NWC', 'WIO', 'NWC'), feature_group_count=CONV_WIDTH)
    return b_gate * y

def first_inputs(seed: int = 0) -> dict:
    key = jax.random.key(seed)
    ks = iter(jax.random.split(key, 64))
    nrm = lambda shape, scale: jax.random.normal(next(ks), shape, jnp.float32) * scale
    gain = lambda shape: 1.0 + nrm(shape, 0.05)
    unif = lambda shape, lo, hi: jax.random.uniform(next(ks), shape, jnp.float32, lo, hi)
    L, Lv = DEPTH, DEPTH - 1
    x = nrm((BATCH, SEQ, D_MODEL), 1.0)
    offsets = jax.random.randint(next(ks), (BATCH, 1), 0, 4096, dtype=jnp.int32)
    positions = offsets + jnp.arange(SEQ, dtype=jnp.int32)[None, :]
    return {
        'x': x,
        'positions': positions,
        'attn_norm': gain((L, D_MODEL)),
        'w_in': nrm((L, D_MODEL, IN_COLS), D_MODEL ** -0.5),
        'mla_q_a_norm': gain((L, Q_LORA_RANK)),
        'mla_wq_b': nrm((L, Q_LORA_RANK, MLA_HEADS * QK_HEAD_DIM), Q_LORA_RANK ** -0.5),
        'mla_kv_a_norm': gain((L, KV_LORA_RANK)),
        'mla_wkv_b': nrm((L, KV_LORA_RANK, MLA_HEADS * (QK_NOPE_DIM + V_HEAD_DIM)), KV_LORA_RANK ** -0.5),
        'mla_q_norm': gain((L, QK_HEAD_DIM)),
        'mla_k_norm': gain((L, QK_HEAD_DIM)),
        'mla_w_o': nrm((L, MLA_HEADS * V_HEAD_DIM, D_MODEL), (MLA_HEADS * V_HEAD_DIM) ** -0.5),
        'rwkv_mu': unif((L, RWKV_COLS), 0.0, 1.0),
        'rwkv_w0': unif((L, RWKV_WIDTH), -6.0, -1.0),
        'rwkv_w2': nrm((L, DECAY_LORA, RWKV_WIDTH), 0.5 * DECAY_LORA ** -0.5),
        'rwkv_a0': nrm((L, RWKV_WIDTH), 0.1),
        'rwkv_a2': nrm((L, AAA_LORA, RWKV_WIDTH), 0.5 * AAA_LORA ** -0.5),
        'rwkv_g2': nrm((L, GATE_LORA, RWKV_WIDTH), GATE_LORA ** -0.5),
        'rwkv_k_k': 0.85 + nrm((L, RWKV_WIDTH), 0.05),
        'rwkv_k_a': gain((L, RWKV_WIDTH)),
        'rwkv_r_k': nrm((L, RWKV_HEADS, RWKV_HEAD_DIM), 0.1),
        'rwkv_ln_w': gain((L, RWKV_WIDTH)),
        'rwkv_ln_b': nrm((L, RWKV_WIDTH), 0.02),
        'rwkv_w_o': nrm((L, RWKV_WIDTH, D_MODEL), RWKV_WIDTH ** -0.5),
        'rwkv_v1': nrm((Lv, D_MODEL, MV_LORA), D_MODEL ** -0.5),
        'rwkv_v_mu': unif((Lv, MV_LORA), 0.0, 1.0),
        'rwkv_v0': nrm((Lv, RWKV_WIDTH), 0.1),
        'rwkv_v2': nrm((Lv, MV_LORA, RWKV_WIDTH), 0.5 * MV_LORA ** -0.5),
        'conv_w': nrm((L, CONV_K, CONV_WIDTH), CONV_K ** -0.5),
        'conv_w_o': nrm((L, CONV_WIDTH, D_MODEL), CONV_WIDTH ** -0.5),
        'w_out': nrm((L, D_MODEL, D_MODEL), D_MODEL ** -0.5),
        'mlp_norm': gain((L, D_MODEL)),
        'w_up': nrm((L, D_MODEL, D_FF), D_MODEL ** -0.5),
        'w_down': nrm((L, D_FF, D_MODEL), D_FF ** -0.5),
    }

def first_block(x, positions, attn_norm, w_in, mla_q_a_norm, mla_wq_b, mla_kv_a_norm, mla_wkv_b,
              mla_q_norm, mla_k_norm, mla_w_o, rwkv_mu, rwkv_w0, rwkv_w2, rwkv_a0, rwkv_a2, rwkv_g2,
              rwkv_k_k, rwkv_k_a, rwkv_r_k, rwkv_ln_w, rwkv_ln_b, rwkv_w_o, rwkv_v1, rwkv_v_mu,
              rwkv_v0, rwkv_v2, conv_w, conv_w_o, w_out, mlp_norm, w_up, w_down):
    bsz, seq, _ = x.shape
    v_first = None
    for l in range(DEPTH):
        h = rms_norm(x, attn_norm[l])
        proj = h @ w_in[l]
        gate_cols, mla_cols, rwkv_cols, conv_cols = _split(proj, [GATE_COLS, MLA_COLS, RWKV_COLS, CONV_COLS])
        o_a = mla_branch(mla_cols, positions, mla_q_a_norm[l], mla_wq_b[l], mla_kv_a_norm[l],
                         mla_wkv_b[l], mla_q_norm[l], mla_k_norm[l]) @ mla_w_o[l]
        vres = None if l == 0 else (rwkv_v1[l - 1], rwkv_v_mu[l - 1], rwkv_v0[l - 1], rwkv_v2[l - 1])
        o_b, v_first = rwkv7_branch(rwkv_cols, h, v_first, rwkv_mu[l], rwkv_w0[l], rwkv_w2[l], rwkv_a0[l],
                                    rwkv_a2[l], rwkv_g2[l], rwkv_k_k[l], rwkv_k_a[l], rwkv_r_k[l],
                                    rwkv_ln_w[l], rwkv_ln_b[l], vres)
        o_b = o_b @ rwkv_w_o[l]
        o_c = short_conv_branch(conv_cols, conv_w[l]) @ conv_w_o[l]
        g = jax.nn.sigmoid(gate_cols).reshape(bsz, seq, N_BRANCH, D_MODEL)
        merged = g[:, :, 0] * o_a + g[:, :, 1] * o_b + g[:, :, 2] * o_c
        x = x + merged @ w_out[l]
        h2 = rms_norm(x, mlp_norm[l])
        x = x + jnp.square(jax.nn.relu(h2 @ w_up[l])) @ w_down[l]
    return x


DEPTH_2 = 4

N_MIXERS = 4
N_CONV_LAYERS = (DEPTH_2 + 3) // 4
N_HGRN_LAYERS = (DEPTH_2 + 2) // 4
N_MLSTM_LAYERS = (DEPTH_2 + 1) // 4
N_SB_LAYERS = DEPTH_2 // 4
D_FF_2 = 2816
FFN_CONV = 3
CONV_WIDTH_2 = 31
HGRN_EXPAND = 128
HGRN_HEADS = D_MODEL // HGRN_EXPAND
HGRN_FDIM = HGRN_HEADS * HGRN_EXPAND
HGRN_VDIM = D_MODEL // HGRN_HEADS
HGRN_CHUNK = 32
MLSTM_INNER = 2 * D_MODEL
MLSTM_HEADS = 4
MLSTM_HDIM = MLSTM_INNER // MLSTM_HEADS
MLSTM_CONV = 4
MLSTM_QKV_BLOCK = 4
MLSTM_CHUNK = 64
SB_HEADS = 16
SB_HDIM = D_MODEL // SB_HEADS
SB_BLOCK = 128
DN_ALPHA = (2.0 * DEPTH_2) ** 0.25
DN_BETA = (8.0 * DEPTH_2) ** -0.25
LN_EPS = 1e-5
RMS_EPS = 1e-6


def layer_norm(x, g, b):
    xf = x.astype(jnp.float32)
    mu = jnp.mean(xf, axis=-1, keepdims=True)
    var = jnp.mean(jnp.square(xf - mu), axis=-1, keepdims=True)
    y = (xf - mu) * lax.rsqrt(var + LN_EPS)
    return (y * g.astype(jnp.float32) + b.astype(jnp.float32)).astype(x.dtype)

def causal_dwconv(x, w, b):
    width = w.shape[0]
    xp = jnp.pad(x, ((0, 0), (width - 1, 0), (0, 0)))
    y = lax.conv_general_dilated(xp, w[:, None, :].astype(x.dtype), window_strides=(1,), padding='VALID',
                                 dimension_numbers=('NWC', 'WIO', 'NWC'), feature_group_count=x.shape[-1])
    return y + b

def adaln(c, w, b):
    m = jax.nn.silu(c) @ w + b
    return [t[:, None, :] for t in jnp.split(m, 6, axis=-1)]

def conformer_conv_module(h, w_pw1, b_pw1, dw_w, dw_b, ln_g, ln_b, w_pw2, b_pw2):
    u = jax.nn.glu(h @ w_pw1 + b_pw1, axis=-1)
    u = causal_dwconv(u, dw_w, dw_b)
    u = jax.nn.silu(layer_norm(u, ln_g, ln_b))
    return u @ w_pw2 + b_pw2

def hgrn2_chunked(q, k, v, log_f):
    B_, S_, H, dk = q.shape
    dv = v.shape[-1]
    C = HGRN_CHUNK
    N = S_ // C

    def to_chunks(t):
        return jnp.moveaxis(t.reshape(B_, N, C, H, t.shape[-1]), 1, 0)

    q, k, v, log_f = map(to_chunks, (q, k, v, log_f))
    b = jnp.cumsum(log_f, axis=2)
    b_ref = b[:, :, C // 2 - 1:C // 2]
    scores = jnp.einsum('nbthd,nbshd->nbhts', q * jnp.exp(b - b_ref), k * jnp.exp(b_ref - b))
    causal = jnp.tril(jnp.ones((C, C), dtype=bool))
    o_intra = jnp.einsum('nbhts,nbshv->nbthv', jnp.where(causal, scores, 0.0), v)
    b_last = b[:, :, -1]
    q_dec = q * jnp.exp(b)
    k_dec = k * jnp.exp(b_last[:, :, None] - b)

    def step(S, inp):
        qd, kd, vc, dec = inp
        o = jnp.einsum('bthd,bhdv->bthv', qd, S)
        S = dec[..., None] * S + jnp.einsum('bshd,bshv->bhdv', kd, vc)
        return S, o

    S0 = jnp.zeros((B_, H, dk, dv), jnp.float32)
    _, o_inter = lax.scan(step, S0, (q_dec, k_dec, v, jnp.exp(b_last)))
    o = o_intra + o_inter
    return jnp.moveaxis(o, 0, 1).reshape(B_, S_, H, dv)

def hgrn2_layer(h, lower_bound, w_in, norm_g, w_out):
    B_, S_, _ = h.shape
    proj = h @ w_in
    q_pre, f_pre, i_val, g_out = jnp.split(proj, [HGRN_FDIM, 2 * HGRN_FDIM, 2 * HGRN_FDIM + D_MODEL], axis=-1)
    lb = lower_bound.astype(jnp.float32)
    q = jax.nn.silu(q_pre.astype(jnp.float32))
    f = lb + (1.0 - lb) * jax.nn.sigmoid(f_pre.astype(jnp.float32))
    k = 1.0 - f
    heads = lambda t: t.reshape(B_, S_, HGRN_HEADS, -1)
    o = hgrn2_chunked(heads(q), heads(k), heads(i_val.astype(jnp.float32)), heads(jnp.log(f)))
    o = o * lax.rsqrt(jnp.mean(jnp.square(o), axis=-1, keepdims=True) + RMS_EPS) * norm_g.astype(jnp.float32)
    o = o.reshape(B_, S_, D_MODEL).astype(h.dtype) * jax.nn.silu(g_out)
    return o @ w_out

def headwise(x, w):
    B_, S_, _ = x.shape
    xg = x.reshape(B_, S_, w.shape[0], w.shape[1])
    return jnp.einsum('bsgi,gio->bsgo', xg, w).reshape(B_, S_, -1)

def mlstm_chunked(q, k, v, i_pre, f_pre):
    B_, S_, H, d = q.shape
    C = MLSTM_CHUNK
    N = S_ // C
    k = k * (d ** -0.5)
    log_f = jax.nn.log_sigmoid(f_pre)

    def to_chunks(t):
        return jnp.moveaxis(t.reshape((B_, N, C) + t.shape[2:]), 1, 0)

    qc, kc, vc, li, lf = map(to_chunks, (q, k, v, i_pre, log_f))
    bc = jnp.cumsum(lf, axis=2)
    causal = jnp.tril(jnp.ones((C, C), dtype=bool))[None, :, :, None]

    def step(carry, inp):
        Cm, n, m = carry
        qt, kt, vt, it, bt = inp
        log_w = bt[:, :, None, :] - bt[:, None, :, :] + it[:, None, :, :]
        log_w = jnp.where(causal, log_w, -jnp.inf)
        log_inter = bt + m[:, None, :]
        m_t = jnp.maximum(jnp.max(log_w, axis=2), log_inter)
        s_qk = jnp.einsum('bthd,bshd->btsh', qt, kt) * jnp.exp(log_w - m_t[:, :, None, :])
        w_inter = jnp.exp(log_inter - m_t)
        num = jnp.einsum('btsh,bshd->bthd', s_qk, vt) + w_inter[..., None] * jnp.einsum('bthd,bhde->bthe', qt, Cm)
        den = jnp.sum(s_qk, axis=2) + w_inter * jnp.einsum('bthd,bhd->bth', qt, n)
        h_out = num / jnp.maximum(jnp.abs(den), jnp.exp(-m_t))[..., None]
        b_last = bt[:, -1]
        log_ws = b_last[:, None, :] - bt + it
        m_new = jnp.maximum(b_last + m, jnp.max(log_ws, axis=1))
        ws = jnp.exp(log_ws - m_new[:, None, :])
        dec = jnp.exp(b_last + m - m_new)
        kw = kt * ws[..., None]
        Cm = dec[..., None, None] * Cm + jnp.einsum('bshd,bshe->bhde', kw, vt)
        n = dec[..., None] * n + jnp.sum(kw, axis=1)
        return (Cm, n, m_new), h_out

    init = (jnp.zeros((B_, H, d, d), jnp.float32), jnp.zeros((B_, H, d), jnp.float32), jnp.zeros((B_, H), jnp.float32))
    _, h_all = lax.scan(step, init, (qc, kc, vc, li, bc))
    return jnp.moveaxis(h_all, 0, 1).reshape(B_, S_, H, d)

def mlstm_layer(h, w_up, conv_w, conv_b, w_q, w_k, w_v, w_gates, b_gates, norm_g, skip, w_down):
    B_, S_, _ = h.shape
    xm, z = jnp.split(h @ w_up, 2, axis=-1)
    xc = jax.nn.silu(causal_dwconv(xm, conv_w, conv_b))
    q = headwise(xc, w_q)
    k = headwise(xc, w_k)
    v = headwise(xm, w_v)
    gates = jnp.concatenate([q, k, v], axis=-1) @ w_gates + b_gates
    i_pre, f_pre = jnp.split(gates.astype(jnp.float32), 2, axis=-1)
    heads = lambda t: t.reshape(B_, S_, MLSTM_HEADS, MLSTM_HDIM).astype(jnp.float32)
    hc = mlstm_chunked(heads(q), heads(k), heads(v), i_pre, f_pre)
    mu = jnp.mean(hc, axis=-1, keepdims=True)
    var = jnp.mean(jnp.square(hc - mu), axis=-1, keepdims=True)
    hc = ((hc - mu) * lax.rsqrt(var + LN_EPS)).reshape(B_, S_, MLSTM_INNER).astype(h.dtype)
    hc = hc * norm_g + skip * xc
    return (hc * jax.nn.silu(z)) @ w_down

def stick_breaking_layer(h, w_qkv, w_out):
    B_, S_, _ = h.shape
    qkv = (h @ w_qkv).reshape(B_, S_, 3, SB_HEADS, SB_HDIM).astype(jnp.float32)
    q = qkv[:, :, 0] * (SB_HDIM ** -0.5)
    k = qkv[:, :, 1]
    v = qkv[:, :, 2]
    blocks = []
    for t0 in range(0, S_, SB_BLOCK):
        t1 = t0 + SB_BLOCK
        z = jnp.einsum('bthd,bshd->bhts', q[:, t0:t1], k[:, :t1])
        valid = jnp.arange(t1)[None, :] < jnp.arange(t0, t1)[:, None]
        neg_log_1mb = jnp.where(valid, jax.nn.softplus(z), 0.0)
        later = lax.cumsum(neg_log_1mb, axis=3, reverse=True) - neg_log_1mb
        a = jnp.where(valid, jnp.exp(jax.nn.log_sigmoid(z) - later), 0.0)
        blocks.append(jnp.einsum('bhts,bshd->bthd', a, v[:, :t1]))
    o = jnp.concatenate(blocks, axis=1).reshape(B_, S_, D_MODEL).astype(h.dtype)
    return o @ w_out

def conv_ffn(h, w_up, conv_w, conv_b, w_down):
    u = causal_dwconv(h @ w_up, conv_w, conv_b)
    gate, val = jnp.split(u, 2, axis=-1)
    return (jax.nn.silu(gate) * val) @ w_down

def second_inputs(seed: int = 0) -> dict:
    key = jax.random.key(seed)
    ks = iter(jax.random.split(key, 48))

    def nrm(shape, scale):
        return scale * jax.random.normal(next(ks), shape, jnp.float32)

    D, F = D_MODEL, D_FF_2
    NA, NB, NC, ND = N_CONV_LAYERS, N_HGRN_LAYERS, N_MLSTM_LAYERS, N_SB_LAYERS
    G = MLSTM_INNER // MLSTM_QKV_BLOCK
    blk = MLSTM_QKV_BLOCK
    b_gates = jnp.concatenate([nrm((NC, MLSTM_HEADS), 0.1),
                               jnp.linspace(3.0, 6.0, MLSTM_HEADS)[None, :] + nrm((NC, MLSTM_HEADS), 0.1)], axis=-1)
    return {
        'x': nrm((BATCH, SEQ, D), 1.0),
        'c': nrm((BATCH, D), 1.0),
        'ada_w': nrm((DEPTH_2, D, 6 * D), 0.1 * D ** -0.5),
        'ada_b': nrm((DEPTH_2, 6 * D), 0.02),
        'post_ln_g': 1.0 + nrm((DEPTH_2, 2, D), 0.05),
        'post_ln_b': nrm((DEPTH_2, 2, D), 0.02),
        'ffn_w_up': nrm((DEPTH_2, D, 2 * F), D ** -0.5),
        'ffn_conv_w': nrm((DEPTH_2, FFN_CONV, 2 * F), FFN_CONV ** -0.5),
        'ffn_conv_b': nrm((DEPTH_2, 2 * F), 0.02),
        'ffn_w_down': nrm((DEPTH_2, F, D), DN_BETA * F ** -0.5),
        'cc_w_pw1': nrm((NA, D, 2 * D), D ** -0.5),
        'cc_b_pw1': nrm((NA, 2 * D), 0.02),
        'cc_dw_w': nrm((NA, CONV_WIDTH_2, D), CONV_WIDTH_2 ** -0.5),
        'cc_dw_b': nrm((NA, D), 0.02),
        'cc_ln_g': 1.0 + nrm((NA, D), 0.05),
        'cc_ln_b': nrm((NA, D), 0.02),
        'cc_w_pw2': nrm((NA, D, D), DN_BETA * D ** -0.5),
        'cc_b_pw2': nrm((NA, D), 0.02),
        'hg_lb_logits': 1.0 + nrm((DEPTH_2, HGRN_FDIM), 0.5),
        'hg_w_in': nrm((NB, D, 2 * HGRN_FDIM + 2 * D), D ** -0.5),
        'hg_norm_g': 1.0 + nrm((NB, HGRN_VDIM), 0.05),
        'hg_w_out': nrm((NB, D, D), DN_BETA * D ** -0.5),
        'ml_w_up': nrm((NC, D, 2 * MLSTM_INNER), D ** -0.5),
        'ml_conv_w': nrm((NC, MLSTM_CONV, MLSTM_INNER), MLSTM_CONV ** -0.5),
        'ml_conv_b': nrm((NC, MLSTM_INNER), 0.02),
        'ml_w_q': nrm((NC, G, blk, blk), blk ** -0.5),
        'ml_w_k': nrm((NC, G, blk, blk), blk ** -0.5),
        'ml_w_v': nrm((NC, G, blk, blk), blk ** -0.5),
        'ml_w_gates': nrm((NC, 3 * MLSTM_INNER, 2 * MLSTM_HEADS), 0.1 * (3 * MLSTM_INNER) ** -0.5),
        'ml_b_gates': b_gates,
        'ml_norm_g': 1.0 + nrm((NC, MLSTM_INNER), 0.05),
        'ml_skip': 1.0 + nrm((NC, MLSTM_INNER), 0.05),
        'ml_w_down': nrm((NC, MLSTM_INNER, D), DN_BETA * MLSTM_INNER ** -0.5),
        'sb_w_qkv': nrm((ND, D, 3 * D), D ** -0.5),
        'sb_w_out': nrm((ND, D, D), DN_BETA * D ** -0.5),
    }

def second_block(x, c, ada_w, ada_b, post_ln_g, post_ln_b,
              ffn_w_up, ffn_conv_w, ffn_conv_b, ffn_w_down,
              cc_w_pw1, cc_b_pw1, cc_dw_w, cc_dw_b, cc_ln_g, cc_ln_b, cc_w_pw2, cc_b_pw2,
              hg_lb_logits, hg_w_in, hg_norm_g, hg_w_out,
              ml_w_up, ml_conv_w, ml_conv_b, ml_w_q, ml_w_k, ml_w_v, ml_w_gates, ml_b_gates,
              ml_norm_g, ml_skip, ml_w_down,
              sb_w_qkv, sb_w_out):
    lb_all = jax.nn.softmax(hg_lb_logits.astype(jnp.float32), axis=0)
    lb_all = jnp.cumsum(lb_all, axis=0) - lb_all[:1]
    for i in range(DEPTH_2):
        kind, j = i % N_MIXERS, i // N_MIXERS
        shift1, scale1, gate1, shift2, scale2, gate2 = adaln(c, ada_w[i], ada_b[i])
        h = x * (1.0 + scale1) + shift1
        if kind == 0:
            y = conformer_conv_module(h, cc_w_pw1[j], cc_b_pw1[j], cc_dw_w[j], cc_dw_b[j],
                                      cc_ln_g[j], cc_ln_b[j], cc_w_pw2[j], cc_b_pw2[j])
        elif kind == 1:
            y = hgrn2_layer(h, lb_all[i], hg_w_in[j], hg_norm_g[j], hg_w_out[j])
        elif kind == 2:
            y = mlstm_layer(h, ml_w_up[j], ml_conv_w[j], ml_conv_b[j], ml_w_q[j], ml_w_k[j], ml_w_v[j],
                            ml_w_gates[j], ml_b_gates[j], ml_norm_g[j], ml_skip[j], ml_w_down[j])
        else:
            y = stick_breaking_layer(h, sb_w_qkv[j], sb_w_out[j])
        x = layer_norm(DN_ALPHA * x + (1.0 + gate1) * y, post_ln_g[i, 0], post_ln_b[i, 0])
        h = x * (1.0 + scale2) + shift2
        y = conv_ffn(h, ffn_w_up[i], ffn_conv_w[i], ffn_conv_b[i], ffn_w_down[i])
        x = layer_norm(DN_ALPHA * x + (1.0 + gate2) * y, post_ln_g[i, 1], post_ln_b[i, 1])
    return x


def setup_inputs(seed=0):
    out = dict(first_inputs(seed))
    for name, value in second_inputs(seed + 1).items():
        if name != "x":
            out[name + "_2"] = value
    return out


def reference(
    x, positions, attn_norm, w_in, mla_q_a_norm, mla_wq_b, mla_kv_a_norm, mla_wkv_b, mla_q_norm,
    mla_k_norm, mla_w_o, rwkv_mu, rwkv_w0, rwkv_w2, rwkv_a0, rwkv_a2, rwkv_g2, rwkv_k_k,
    rwkv_k_a, rwkv_r_k, rwkv_ln_w, rwkv_ln_b, rwkv_w_o, rwkv_v1, rwkv_v_mu, rwkv_v0, rwkv_v2,
    conv_w, conv_w_o, w_out, mlp_norm, w_up, w_down, c_2, ada_w_2, ada_b_2, post_ln_g_2,
    post_ln_b_2, ffn_w_up_2, ffn_conv_w_2, ffn_conv_b_2, ffn_w_down_2, cc_w_pw1_2, cc_b_pw1_2,
    cc_dw_w_2, cc_dw_b_2, cc_ln_g_2, cc_ln_b_2, cc_w_pw2_2, cc_b_pw2_2, hg_lb_logits_2,
    hg_w_in_2, hg_norm_g_2, hg_w_out_2, ml_w_up_2, ml_conv_w_2, ml_conv_b_2, ml_w_q_2, ml_w_k_2,
    ml_w_v_2, ml_w_gates_2, ml_b_gates_2, ml_norm_g_2, ml_skip_2, ml_w_down_2, sb_w_qkv_2,
    sb_w_out_2,
):
    x = first_block(
        x, positions, attn_norm, w_in, mla_q_a_norm, mla_wq_b, mla_kv_a_norm, mla_wkv_b,
        mla_q_norm, mla_k_norm, mla_w_o, rwkv_mu, rwkv_w0, rwkv_w2, rwkv_a0, rwkv_a2, rwkv_g2,
        rwkv_k_k, rwkv_k_a, rwkv_r_k, rwkv_ln_w, rwkv_ln_b, rwkv_w_o, rwkv_v1, rwkv_v_mu,
        rwkv_v0, rwkv_v2, conv_w, conv_w_o, w_out, mlp_norm, w_up, w_down,
    )
    return second_block(
        x, c_2, ada_w_2, ada_b_2, post_ln_g_2, post_ln_b_2, ffn_w_up_2, ffn_conv_w_2,
        ffn_conv_b_2, ffn_w_down_2, cc_w_pw1_2, cc_b_pw1_2, cc_dw_w_2, cc_dw_b_2, cc_ln_g_2,
        cc_ln_b_2, cc_w_pw2_2, cc_b_pw2_2, hg_lb_logits_2, hg_w_in_2, hg_norm_g_2, hg_w_out_2,
        ml_w_up_2, ml_conv_w_2, ml_conv_b_2, ml_w_q_2, ml_w_k_2, ml_w_v_2, ml_w_gates_2,
        ml_b_gates_2, ml_norm_g_2, ml_skip_2, ml_w_down_2, sb_w_qkv_2, sb_w_out_2,
    )


_drawn_inputs = setup_inputs


def setup_inputs(seed=0):
    import zlib

    import numpy as np

    out = dict(_drawn_inputs(seed))
    spreads = {}
    factors = {'mla_q_a_norm': 8.0,
     'mla_kv_a_norm': 4.709,
     'mla_q_norm': 7.91,
     'mla_k_norm': 8.0,
     'rwkv_w2': 4.899,
     'rwkv_a0': 3.551,
     'rwkv_k_k': 3.542,
     'rwkv_k_a': 2.685,
     'rwkv_ln_w': 3.17,
     'rwkv_ln_b': 7.543,
     'rwkv_v_mu': 3.002,
     'rwkv_v0': 6.682,
     'ffn_conv_b_2': 6.168,
     'cc_b_pw1_2': 8.0,
     'cc_dw_b_2': 8.0,
     'cc_ln_g_2': 8.0,
     'cc_ln_b_2': 25.398,
     'cc_b_pw2_2': 8.0,
     'hg_lb_logits_2': 8.0,
     'hg_norm_g_2': 8.0,
     'ml_conv_b_2': 8.0,
     'ml_w_gates_2': 7.732,
     'ml_norm_g_2': 7.789,
     'ml_skip_2': 8.0}
    for name, (base, spread) in spreads.items():
        noise = np.random.default_rng([zlib.crc32(name.encode()), seed]).standard_normal(out[name].shape)
        drawn = base * np.exp(spread * noise) if base else spread * noise
        out[name] = jnp.asarray(drawn.astype(out[name].dtype))
    for name, factor in factors.items():
        out[name] = (out[name] * factor).astype(out[name].dtype)
    return out
```

```python
from contextlib import ExitStack, contextmanager

import numpy as np

import concourse.bass as bass
from concourse import mybir

F32 = mybir.dt.float32
I32 = mybir.dt.int32
ALU = mybir.AluOpType
ACT = mybir.ActivationFunctionType
AX = mybir.AxisListType

P = 128
T = 256
NT = T // P
D = 1024
KD = D // P

L1 = 2
H_MLA, D_NOPE, D_ROPE, D_V = 8, 64, 32, 64
D_QK = D_NOPE + D_ROPE
R_Q, R_KV = 384, 256
H_RW, D_RW = 4, 64
W_RW = H_RW * D_RW
R_DECAY, R_AAA, R_GATE, R_MV = 64, 64, 128, 32
D_CONV = 256
F1 = 4 * D
OFF_MLA = 3 * D
OFF_RW = OFF_MLA + R_Q + R_KV + D_ROPE
OFF_CONV = OFF_RW + 3 * W_RW + R_DECAY + R_AAA + R_GATE
GN_EPS = 64e-5
RMS_EPS = 1e-6
LN_EPS = 1e-5
ROPE_THETA = 10000.0

L2 = 4
F2 = 2816
KF = F2 // P
TAPS_CC, TAPS_FFN, TAPS_ML = 31, 3, 4
H_HG, C_HG = 8, 32
I_ML, H_ML, D_ML = 2 * D, 4, 512
K_ML = I_ML // P
H_SB, D_SB = 16, 64
ALPHA = (2.0 * L2) ** 0.25

UNIT = 4096
RING = 4
ARENA = 26624
BANK = 512

MAGIC = 12582912.0
TWO_PI = 2.0 * np.pi
PI2_HI = 6.28125
PI2_MID = float(np.float32(round((TWO_PI - PI2_HI) * 2**21) / 2**21))
PI2_LO = float(np.float32(TWO_PI - PI2_HI - PI2_MID))
PI = float(np.nextafter(np.float32(np.pi), np.float32(0)))
BIG = 3.0e38
NEG = -1.0e30

H0, OA, OB, OC, WORK = (n * KD * T for n in range(5))
V_FIRST = ARENA - H_RW * T



class Block:

    def __init__(self, array, lead, rows, cols, diagonal=False):
        self.array, self.lead, self.rows, self.cols, self.diagonal = array, lead, rows, cols, diagonal
        self.height = rows[1] - rows[0]
        self.width = P if diagonal else sum(b - a for a, b in cols)
        self.unit = self.at = 0
        self.ends_unit = False
        self.side = False


class SideUnit(Block):

    def __init__(self, lead, index):
        super().__init__("ada_w_2", (lead,), (0, P), [(0, UNIT)])
        self.width, self.side, self.ends_unit, self.index = UNIT, True, True, index

    def pieces(self):
        at, out = self.index * UNIT, []
        while at < (self.index + 1) * UNIT:
            k, c = divmod(at, 6 * D)
            n = min(6 * D - c, (self.index + 1) * UNIT - at)
            out.append((k, c, at - self.index * UNIT, n))
            at += n
        return out


N_SIDE = KD * 6 * D // UNIT


def with_sides(blocks, sides):
    out, n = [], 0
    for k, b in enumerate(blocks):
        while n < len(sides) and n * len(blocks) <= k * len(sides):
            out.append(sides[n])
            n += 1
        out.append(b)
    return out + sides[n:]


def matrix(array, lead, n_rows, columns, row0=0, step=P):
    return [Block(array, lead, (row0 + r, row0 + min(r + step, n_rows)), [c] if isinstance(c, tuple) else c)
            for c in columns for r in range(0, n_rows, step)]


def tiles(start, count, width=P):
    return [(start + i * width, start + (i + 1) * width) for i in range(count)]


def weight_order():
    g = {}
    for l in range(L1):
        g["mla_in", l] = matrix("w_in", (l,), D, tiles(OFF_MLA, (R_Q + R_KV) // P)
                                + [(OFF_MLA + R_Q + R_KV, OFF_MLA + R_Q + R_KV + D_ROPE)])
        g["wq_b", l] = matrix("mla_wq_b", (l,), R_Q, tiles(0, H_MLA, D_QK))
        g["wk_b", l] = matrix("mla_wkv_b", (l,), R_KV, [(h * P, h * P + D_NOPE) for h in range(H_MLA)])
        g["wv_b", l] = matrix("mla_wkv_b", (l,), R_KV,
                              [[(h * P + D_NOPE, (h + 1) * P) for h in range(H_MLA)]])
        g["mla_o", l] = matrix("mla_w_o", (l,), H_MLA * D_V, tiles(0, KD))
        g["rwkv_in", l] = matrix("w_in", (l,), D, tiles(OFF_RW, 3 * H_RW + 2, D_RW)
                                 + [(OFF_RW + 3 * W_RW + 128, OFF_RW + 3 * W_RW + 256)])
        if l:
            g["v1", l] = matrix("rwkv_v1", (l - 1,), D, [(0, R_MV)])
        g["w2", l] = matrix("rwkv_w2", (l,), R_DECAY, tiles(0, H_RW, D_RW))
        g["a2", l] = matrix("rwkv_a2", (l,), R_AAA, tiles(0, H_RW, D_RW))
        if l:
            g["v2", l] = matrix("rwkv_v2", (l - 1,), R_MV, tiles(0, H_RW, D_RW))
        g["g2", l] = matrix("rwkv_g2", (l,), R_GATE, tiles(0, H_RW, D_RW))
        g["rwkv_o", l] = matrix("rwkv_w_o", (l,), W_RW, tiles(0, KD), step=D_RW)
        g["conv_in", l] = matrix("w_in", (l,), D, tiles(OFF_CONV, 6))
        g["conv_o", l] = matrix("conv_w_o", (l,), D_CONV, tiles(0, KD))
        g["gates", l] = [b for m in range(KD) for i in range(3)
                         for b in matrix("w_in", (l,), D, tiles(i * D + m * P, 1))]
        sides = [[SideUnit(2 * l + j, n) for n in range(N_SIDE)] for j in range(2)]
        g["w_out", l] = with_sides(matrix("w_out", (l,), D, tiles(0, KD)), sides[0][:2])
        g["up", l] = with_sides(matrix("w_up", (l,), D, tiles(0, F1 // P)), sides[0][2:])
        g["down", l] = with_sides(matrix("w_down", (l,), F1, tiles(0, KD)), sides[1])
    for i in range(L2):
        if i == 0:
            g["pw1", i] = [b for m in range(KD) for half in range(2)
                           for b in matrix("cc_w_pw1_2", (0,), D, tiles(half * D + m * P, 1))]
            g["pw2", i] = matrix("cc_w_pw2_2", (0,), D, tiles(0, KD))
        if i == 1:
            g["hg_q", i] = matrix("hg_w_in_2", (0,), D, tiles(0, KD))
            g["hg_f", i] = matrix("hg_w_in_2", (0,), D, tiles(D, KD))
            g["hg_v", i] = matrix("hg_w_in_2", (0,), D, tiles(2 * D, 2, BANK))
            g["hg_g", i] = matrix("hg_w_in_2", (0,), D, tiles(3 * D, KD))
            g["hg_out", i] = matrix("hg_w_out_2", (0,), D, tiles(0, KD))
        if i == 2:
            g["ml_x", i] = matrix("ml_w_up_2", (0,), D, tiles(0, K_ML))
            for name in "qkv":
                g["ml_" + name, i] = [Block(f"ml_w_{name}_2", (0,), (c * P // 4, (c + 1) * P // 4), None, True)
                                      for c in range(K_ML)]
                for b in g["ml_" + name, i]:
                    b.height = P
            g["ml_z", i] = matrix("ml_w_up_2", (0,), D, tiles(I_ML, K_ML))
            g["ml_down", i] = matrix("ml_w_down_2", (0,), I_ML, tiles(0, KD))
        if i == 3:
            g["sb_qk", i] = matrix("sb_w_qkv_2", (0,), D, tiles(0, 2 * KD))
            g["sb_v", i] = matrix("sb_w_qkv_2", (0,), D, tiles(2 * D, 2, BANK))
            g["sb_out", i] = matrix("sb_w_out_2", (0,), D, tiles(0, KD))
        g["ffn_up", i] = [b for m in range(KF) for half in range(2)
                          for b in matrix("ffn_w_up_2", (i,), D, tiles(half * F2 + m * P, 1))]
        g["ffn_down", i] = matrix("ffn_w_down_2", (i,), F2, tiles(0, KD))
    return g


def place_weights(groups):
    unit = at = 0
    units = 1
    last = None
    for blocks in groups.values():
        for b in blocks:
            if b.side:
                b.unit, units = units, units + 1
                continue
            if at + b.width > UNIT:
                last.ends_unit = True
                unit, at, units = units, 0, units + 1
            b.unit, b.at = unit, at
            at += b.width
            last = b
    last.ends_unit = True
    return units


class Columns:

    def __init__(self):
        self.n, self.at, self.parts = 0, {}, []

    def add(self, name, array, index, n, rows=P):
        self.at[name] = (self.n, n)
        self.parts.append((array, index, n, rows, self.n))
        self.n += n


def parameter_columns():
    c = Columns()
    for l in range(L1):
        c.add(("attn_norm", l), "attn_norm", (l,), KD)
        c.add(("mlp_norm", l), "mlp_norm", (l,), KD)
        c.add(("q_a", l), "mla_q_a_norm", (l,), R_Q // P)
        c.add(("kv_a", l), "mla_kv_a_norm", (l,), R_KV // P)
        c.add(("q_norm", l), "mla_q_norm", (l,), 1, D_QK)
        c.add(("k_norm", l), "mla_k_norm", (l,), 1, D_QK)
        c.add(("mu", l), "rwkv_mu", (l, slice(0, 3 * W_RW + 128)), 3 * H_RW + 2, D_RW)
        c.add(("mu_g", l), "rwkv_mu", (l, slice(3 * W_RW + 128, None)), 1)
        for name in ("w0", "a0", "k_k", "k_a", "r_k", "ln_w", "ln_b"):
            c.add((name, l), "rwkv_" + name, (l,), H_RW, D_RW)
        if l:
            c.add(("v_mu", l), "rwkv_v_mu", (l - 1,), 1, R_MV)
            c.add(("v0", l), "rwkv_v0", (l - 1,), H_RW, D_RW)
        c.add(("conv_w", l), "conv_w", (l,), 3 * D_CONV // P)
    c.add("c", "c_2", (0,), KD)
    for i in range(L2):
        c.add(("ada_b", i), "ada_b_2", (i,), 6 * KD)
        for j in range(2):
            c.add(("post_g", i, j), "post_ln_g_2", (i, j), KD)
            c.add(("post_b", i, j), "post_ln_b_2", (i, j), KD)
        c.add(("ffn_w", i), "ffn_conv_w_2", (i,), TAPS_FFN * 2 * KF)
        c.add(("ffn_b", i), "ffn_conv_b_2", (i,), 2 * KF)
    c.add("b_pw1", "cc_b_pw1_2", (0,), 2 * KD)
    c.add("dw_w", "cc_dw_w_2", (0,), TAPS_CC * KD)
    c.add("dw_b", "cc_dw_b_2", (0,), KD)
    c.add("cc_g", "cc_ln_g_2", (0,), KD)
    c.add("cc_b", "cc_ln_b_2", (0,), KD)
    c.add("b_pw2", "cc_b_pw2_2", (0,), KD)
    c.add("lb", "hg_lb_logits_2", (), L2 * KD)
    c.add("hg_norm", "hg_norm_g_2", (0,), 1)
    c.add("ml_w", "ml_conv_w_2", (0,), TAPS_ML * K_ML)
    c.add("ml_b", "ml_conv_b_2", (0,), K_ML)
    c.add("ml_norm", "ml_norm_g_2", (0,), K_ML)
    c.add("ml_skip", "ml_skip_2", (0,), K_ML)
    c.add("b_if", "ml_b_gates_2", (0,), 2, H_ML)
    c.parts.append(("ml_w_gates_2", (0,), 3 * K_ML, None, c.n))
    c.at["w_if"] = (c.n, 3 * K_ML * 2 * H_ML)
    c.n += 3 * K_ML * 2 * H_ML
    return c


N_LEVELS = 7


def shape_constants():
    i = np.arange(P)
    p, f = i[:, None], i[None, :]
    parts = {
        "ident": p == f,
        "ones": np.ones((P, P)),
        "causal_add": np.where(f <= p, 0.0, NEG),
        "incl": np.concatenate([p <= f, np.ones((P, P)), p <= f], 1),
        "strict": np.concatenate([p < f, np.ones((P, P)), p < f], 1),
        "from_here": p >= f,
        "chunk": (p <= f) & (p // C_HG == f // C_HG),
        "rot": np.zeros((P, P)),
        "sel": np.zeros((P, H_ML * P + 2 * H_ML)),
        "freq": np.zeros((P, 1)),
    }
    for n in range(N_LEVELS):
        w = 1 << n
        parts["level", n] = (p // (2 * w) == f // (2 * w)) & (p % (2 * w) < w) & (f % (2 * w) >= w)
    half = D_ROPE // 2
    for k in range(half):
        parts["rot"][D_NOPE + half + k, D_NOPE + k] = -1.0
        parts["rot"][D_NOPE + k, D_NOPE + half + k] = 1.0
        parts["freq"][[D_NOPE + k, D_NOPE + half + k], 0] = np.float32(ROPE_THETA ** (-(k * 2.0 / D_ROPE)))
    for h in range(H_ML):
        parts["sel"][h, h * P:(h + 1) * P] = 1.0
        parts["sel"][h, H_ML * P + h] = 1.0
        parts["sel"][H_ML + h, H_ML * P + H_ML + h] = 1.0
    at, n = {}, 0
    for name, a in parts.items():
        at[name] = (n, a.shape[1])
        n += a.shape[1]
    return at, np.concatenate([np.asarray(a, np.float32) for a in parts.values()], 1)



class Chip:

    def __init__(self, nc, ctx, stream, groups, columns, constants, n_units):
        self.nc, self.stream, self.groups, self.columns, self.constants = nc, stream, groups, columns, constants
        self.n_units = n_units

        def sb(name, n, dt=F32):
            return ctx.enter_context(nc.sbuf_tensor(name, [P, n], dt))

        self.ring = sb("ring", RING * UNIT)
        self.x = sb("x", KD * T)
        self.cols = sb("cols", columns.n)
        self.const = sb("const", sum(n for _, n in constants.values()))
        self.ada = sb("ada", L2 * 6 * KD)
        self.small = sb("small", 160)
        self.stat = sb("stat", 8 * T)
        self.cos, self.sin, self.pos = sb("cos", T), sb("sin", T), sb("pos", T, I32)
        self.arena = sb("arena", ARENA)
        self.silu_c = self.small[:, 112:120]
        self.lb, self.lb_rest = self.small[:, 48:56], self.small[:, 56:64]
        self.ada_sums = [self.place(OA, 6 * D), self.place(WORK + F1 // P * T + 2048, 6 * D)]
        self.psum = ctx.enter_context(nc.psum_tensor("psum", [P, 8 * BANK], F32))
        self.semaphores = Semaphores(nc, ctx)
        self.out_written = ctx.enter_context(nc.semaphore("out_written"))
        self.loaded = [ctx.enter_context(nc.semaphore(f"unit_loaded_{i}")) for i in range(RING)]

    def col(self, name, k=0, n=1, rows=P):
        at, count = self.columns.at[name]
        assert k + n <= count
        return self.cols[0:rows, at + k:at + k + n]

    def con(self, name, rows=P, cols=None):
        at, n = self.constants[name]
        return self.const[0:rows, at:at + (cols or n)]

    def bank(self, i, n=BANK, rows=P, at=0):
        return self.psum[0:rows, i * BANK + at:i * BANK + at + n]

    def place(self, at, *dims, rows=P):
        n = int(np.prod(dims))
        assert at + n <= ARENA, (at, dims)
        ap = self.arena[0:rows, at:at + n]
        if len(dims) == 2:
            ap = ap.rearrange("p (a b) -> p a b", b=dims[1])
        elif len(dims) == 3:
            ap = ap.rearrange("p (a b c) -> p a b c", b=dims[1], c=dims[2])
        return ap


    def load_unit(self, sp, u):
        slot = u % RING
        sp.dma_start(self.ring[:, slot * UNIT:(slot + 1) * UNIT], self.stream[u]).then_inc(self.loaded[slot], 16)

    def weight(self, b):
        return self.ring[0:b.height, (b.unit % RING) * UNIT + b.at:(b.unit % RING) * UNIT + b.at + b.width]

    def arrived(self, pe, blocks, k):
        b = blocks[k]
        if k == 0 or blocks[k - 1].unit != b.unit:
            pe.wait_ge(self.loaded[b.unit % RING], 16 * (b.unit // RING + 1))

    def refill(self, sp, blocks, per_step, steps_done, sides=(), sides_done=None):
        ended = [(b.unit, steps_done, k // per_step + 1) for k, b in enumerate(blocks) if b.ends_unit]
        ended += [(b.unit, sides_done, n + 1) for n, b in enumerate(sides)]
        for unit, done, count in sorted(ended, key=lambda e: e[0]):
            if unit + RING < self.n_units:
                sp.wait_ge(done, count)
                self.load_unit(sp, unit + RING)


class Semaphores:

    SIZE = 10

    def __init__(self, nc, ctx):
        self.sets = [[ctx.enter_context(nc.semaphore(f"stage_{s}_{i}")) for i in range(self.SIZE)] for s in "ab"]
        self.turn = 0


@contextmanager
def stage(chip, *names):
    used, other = chip.semaphores.sets[chip.semaphores.turn], chip.semaphores.sets[1 - chip.semaphores.turn]
    chip.semaphores.turn = 1 - chip.semaphores.turn
    with chip.nc.Block(no_gpsimd_drain=True) as block:
        assert len(names) <= len(used)

        @block.gpsimd
        def _(pool):
            pool.sem_clear(range(other[0].num, other[-1].num + 1))

        yield (block, *used[:len(names)])


class Chain:

    def __init__(self, eng, done):
        self.eng, self.done, self.counts = eng, done, {}

    def __call__(self, ins, done=None):
        done = done or self.done
        self.counts[done.num] = self.counts.get(done.num, 0) + 1
        ins.then_inc(done, 1)
        self.eng.wait_ge(done, self.counts[done.num])


def spread(ap, *dims):
    for _ in dims:
        ap = ap.unsqueeze(len(ap.shape))
    return ap.broadcast_to(list(ap.shape[:len(ap.shape) - len(dims)]) + list(dims))


def over(ap, n):
    ap = ap.unsqueeze(1)
    return ap.broadcast_to([ap.shape[0], n] + list(ap.shape[2:]))


def project(chip, name, rhs, nk, epilogue, per=1, out=None):
    blocks = [b for b in chip.groups[name] if not b.side]
    sides = [b for b in chip.groups[name] if b.side]
    steps = len(blocks) // nk // per
    depth = 8 // per if per > 1 else 4

    def banks(i):
        return [chip.bank((i % depth) * per + j, T) for j in range(per)]

    with stage(chip, "tiles_ready", "banks_free", "act_done", "dve_done", "act_chain", "dve_chain", "sides_done") as \
            (block, ready, free, act_done, dve_done, act_chain, dve_chain, sides_done):

        @block.sync
        def _(sp):
            chip.refill(sp, blocks, nk * per, ready, sides, sides_done)

        def side_work(dve, step):
            for n in range(step * len(sides) // steps, (step + 1) * len(sides) // steps):
                b = sides[n]
                dve.wait_ge(chip.loaded[b.unit % RING], 16 * (b.unit // RING + 1))
                if n:
                    dve.wait_ge(sides_done, n)
                at = (b.unit % RING) * UNIT
                for k, c, place, count in b.pieces():
                    acc, w = chip.ada_sums[b.lead[0] % 2][:, c:c + count], chip.ring[:, at + place:at + place + count]
                    if k == 0:
                        ins = dve.tensor_scalar(acc, w, chip.silu_c[:, 0:1], None, ALU.mult)
                    else:
                        ins = dve.scalar_tensor_tensor(acc, w, chip.silu_c[:, k:k + 1], acc, ALU.mult, ALU.add)
                ins.then_inc(sides_done, 1)

        @block.tensor
        def _(pe):
            for i in range(steps):
                if i >= depth:
                    pe.wait_ge(free, i - depth + 1)
                for j in range(per):
                    dst = banks(i)[j]
                    for k in range(nk):
                        n = (i * per + j) * nk + k
                        b = blocks[n]
                        chip.arrived(pe, blocks, n)
                        o = dst[0:b.width] if out is None else out(i, dst, b)
                        ins = pe.matmul(o, chip.weight(b), rhs(i, k), start=(k == 0), stop=(k == nk - 1))
                ins.then_inc(ready, 1)

        epilogue(block, dict(ready=ready, free=free, act_done=act_done, dve_done=dve_done,
                             act_chain=act_chain, dve_chain=dve_chain, side_work=side_work), banks, steps)


def store_with_act(dst, rows=lambda i: P, bias=None):
    def epilogue(block, s, banks, steps):
        @block.scalar
        def _(act):
            for i in range(steps):
                act.wait_ge(s["ready"], i + 1)
                d = dst(i)
                lo = d.base_partition()
                act.activation(d, banks(i)[0][lo:lo + d.shape[0]], ACT.Identity,
                               bias=bias(i) if bias else 0.0).then_inc(s["free"], 1)
    return epilogue


def project_tokens(chip, name, src, nk, dst):
    blocks = chip.groups[name]
    n_groups = len(blocks) // nk
    with stage(chip, "groups_ready", "banks_free") as (block, ready, free):

        @block.sync
        def _(sp):
            chip.refill(sp, blocks, nk, ready)

        @block.tensor
        def _(pe):
            for n in range(n_groups):
                for k in range(nk):
                    b = blocks[n * nk + k]
                    chip.arrived(pe, blocks, n * nk + k)
                    for tt in range(NT):
                        ins = pe.matmul(chip.bank(n * NT + tt, b.width), src(k)[:, tt * P:(tt + 1) * P],
                                        chip.weight(b), start=(k == 0), stop=(k == nk - 1))
                ins.then_inc(ready, 1)

        @block.scalar
        def _(act):
            for n in range(n_groups):
                act.wait_ge(ready, n + 1)
                act.activation(dst(0, n), chip.bank(n * NT, blocks[n * nk].width), ACT.Identity).then_inc(free, 1)

        @block.vector
        def _(dve):
            for n in range(n_groups):
                dve.wait_ge(ready, n + 1)
                dve.tensor_copy(dst(1, n), chip.bank(n * NT + 1, blocks[n * nk].width)).then_inc(free, 1)


def norm(chip, src, dst, scratch, groups, n, rows, eps, gain=None, bias=None, center=False):
    size = float(n * rows)
    width = groups * T
    rstd = chip.stat[0:rows, 0:width]
    sums = lambda at: chip.psum[0:rows, at:at + width]
    mean_at, var_at = 0, 4 * BANK
    with stage(chip, "centred", "squared", "sums_ready", "var_ready", "root_ready", "scaled",
               "dve_chain", "act_chain") as \
            (block, centred, squared, summed, var_ready, root_ready, scaled, dve_chain, act_chain):

        def column_sums(pe, ap, at):
            for g in range(groups):
                for k in range(n):
                    ins = pe.matmul(sums(at + 0)[:, g * T:(g + 1) * T], chip.con("ones", rows, rows),
                                    ap[:, g * n + k, :], start=(k == 0), stop=(k == n - 1))
            ins.then_inc(summed, 1)

        @block.tensor
        def _(pe):
            if center:
                column_sums(pe, src, mean_at)
            pe.wait_ge(squared, 1)
            column_sums(pe, scratch, var_at)

        @block.vector
        def _(dve):
            chain = Chain(dve, dve_chain)
            source = src
            if center:
                dve.wait_ge(summed, 1)
                chain(dve.tensor_scalar(rstd, sums(mean_at), 1.0 / size, None, ALU.mult))
                for g in range(groups):
                    sl = slice(g * n, (g + 1) * n)
                    ins = dve.tensor_tensor(dst[:, sl, :], src[:, sl, :],
                                            over(rstd[:, g * T:(g + 1) * T], n), ALU.subtract)
                    chain(ins)
                source = dst
            dve.tensor_tensor(scratch, source, source, ALU.mult).then_inc(squared, 1)
            dve.wait_ge(summed, 2 if center else 1)
            chain(dve.tensor_scalar(rstd, sums(var_at), 1.0 / size, eps, ALU.mult, ALU.add))
            dve.reciprocal(rstd, rstd).then_inc(var_ready, 1)
            dve.wait_ge(root_ready, 1)
            for g in range(groups):
                sl = slice(g * n, (g + 1) * n)
                dve.tensor_tensor(dst[:, sl, :], source[:, sl, :],
                                  over(rstd[:, g * T:(g + 1) * T], n), ALU.mult).then_inc(scaled, 1)

        @block.scalar
        def _(act):
            act.wait_ge(var_ready, 1)
            act.activation(rstd, rstd, ACT.Sqrt).then_inc(root_ready, 1)
            if gain is None:
                return
            for g in range(groups):
                act.wait_ge(scaled, g + 1)
                for k in range(g * n, (g + 1) * n):
                    act.activation(dst[:, k, :], dst[:, k, :], ACT.Identity, scale=gain(k),
                                   bias=bias(k) if bias else 0.0)



def load_inputs(chip, x_in, cols_in, const_in, positions):
    with stage(chip, "inputs_loaded") as (block, inputs_loaded):

        @block.sync
        def _(sp):
            for u in range(min(RING, chip.n_units)):
                chip.load_unit(sp, u)

        @block.scalar
        def _(act):
            act.dma_start(chip.const[:, :], const_in).then_inc(inputs_loaded, 16)
            act.dma_start(chip.x[:, :], x_in).then_inc(inputs_loaded, 16)
            act.dma_start(chip.cols[:, :], cols_in).then_inc(inputs_loaded, 16)
            act.dma_start(chip.pos[D_NOPE:D_QK, :],
                          positions.broadcast_to([D_ROPE, T])).then_inc(inputs_loaded, 16)
            act.wait_ge(inputs_loaded, 64)

    with stage(chip, "dve_chain", "angles_ready") as (block, dve_chain, angles_ready):
        lo, hi = D_NOPE, D_QK
        ang = chip.place(0, T)[lo:hi]
        turns = chip.place(T, T)[lo:hi]
        cos, sin = chip.cos[lo:hi, :], chip.sin[lo:hi, :]

        @block.vector
        def _(dve):
            chain = Chain(dve, dve_chain)
            dve.memset(chip.cos[0:lo, :], 1.0)
            dve.memset(chip.sin[0:lo, :], 0.0)
            chain(dve.tensor_copy(ang, chip.pos[lo:hi, :]))
            at = chip.constants["freq"][0]
            chain(dve.tensor_scalar(ang, ang, chip.const[lo:hi, at:at + 1], None, ALU.mult))
            for table, quarter in ((sin, 0.0), (cos, 0.25)):
                chain(dve.tensor_scalar(turns, ang, 1.0 / TWO_PI, quarter, ALU.mult, ALU.add))
                chain(dve.tensor_scalar(turns, turns, MAGIC, None, ALU.add))
                chain(dve.tensor_scalar(turns, turns, -MAGIC, None, ALU.add))
                chain(dve.scalar_tensor_tensor(table, turns, -PI2_HI, ang, ALU.mult, ALU.add))
                chain(dve.scalar_tensor_tensor(table, turns, -PI2_MID, table, ALU.mult, ALU.add))
                chain(dve.scalar_tensor_tensor(table, turns, -PI2_LO, table, ALU.mult, ALU.add))
                if quarter:
                    chain(dve.tensor_scalar(table, table, float(np.pi / 2), None, ALU.add))
                chain(dve.tensor_scalar(table, table, -PI, PI, ALU.max, ALU.min))
            dve.tensor_copy(turns, ang).then_inc(angles_ready, 1)

        @block.scalar
        def _(act):
            act.wait_ge(angles_ready, 1)
            act.activation(sin, sin, ACT.Sin)
            act.activation(cos, cos, ACT.Sin)




def mla_branch(chip, l):
    h = chip.place(H0, KD, T)
    cq, ckv = chip.place(WORK, 3, T), chip.place(WORK + 768, 2, T)
    kpe = chip.place(WORK + 1280, T)
    q, k = chip.place(WORK + 1536, H_MLA, T, rows=D_QK), chip.place(WORK + 3584, H_MLA, T, rows=D_QK)
    v = chip.place(WORK + 5632, NT, H_MLA * D_V)
    o = chip.place(WORK + 6656, H_MLA // 2, T)
    scratch = WORK + 7680

    def latent(i):
        return cq[:, i, :] if i < 3 else ckv[:, i - 3, :] if i < 5 else kpe[D_NOPE:D_QK, :]
    project(chip, ("mla_in", l), lambda i, k: h[:, k, :], KD, store_with_act(latent),
            out=lambda i, bank, b: bank if i < 5 else bank[D_NOPE:D_QK])
    norm(chip, cq, cq, chip.place(scratch, 3, T), 1, 3, P, RMS_EPS, gain=lambda k: chip.col(("q_a", l), k))
    norm(chip, ckv, ckv, chip.place(scratch, 2, T), 1, 2, P, RMS_EPS, gain=lambda k: chip.col(("kv_a", l), k))
    project(chip, ("wq_b", l), lambda i, k: cq[:, k, :], 3, store_with_act(lambda i: q[:, i, :]))
    project(chip, ("wk_b", l), lambda i, k: ckv[:, k, :], 2, store_with_act(lambda i: k[0:D_NOPE, i, :]))
    project_tokens(chip, ("wv_b", l), lambda k: ckv[:, k, :], 2, lambda tt, n: v[:, tt, :])
    with stage(chip) as (block,):
        @block.vector
        def _(dve):
            dve.tensor_copy(k[D_NOPE:D_QK], over(kpe[D_NOPE:D_QK, :], H_MLA))

    for x, gain in ((q, "q_norm"), (k, "k_norm")):
        norm(chip, x, x, chip.place(scratch, H_MLA, T, rows=D_QK), H_MLA, 1, D_QK, RMS_EPS,
             gain=lambda j, gain=gain: chip.col((gain, l), rows=D_QK))
        flat = x.rearrange("p h t -> p (h t)")
        turned = chip.place(scratch, H_MLA, T, rows=D_QK)
        with stage(chip, "turned_ready", "dve_chain") as (block, turned_ready, dve_chain):
            @block.tensor
            def _(pe):
                for n in range(4):
                    ins = pe.matmul(chip.bank(n, rows=D_QK), chip.con("rot", D_QK, D_QK),
                                    flat[:, n * BANK:(n + 1) * BANK], start=True, stop=True)
                ins.then_inc(turned_ready, 1)

            @block.vector
            def _(dve):
                chain = Chain(dve, dve_chain)
                dve.wait_ge(turned_ready, 1)
                psum = chip.psum[0:D_QK, 0:4 * BANK].rearrange("p (h t) -> p h t", t=T)
                dve.tensor_tensor(turned, psum, over(chip.sin[0:D_QK, :], H_MLA), ALU.mult)
                chain(dve.tensor_tensor(x, x, over(chip.cos[0:D_QK, :], H_MLA), ALU.mult))
                dve.tensor_tensor(x, x, turned, ALU.add)

    n0, n1 = H_MLA * P, H_MLA * T
    s_at, pt_at = scratch + 2048, scratch + 2048 + n0 + n1
    s0 = chip.place(s_at, H_MLA, P)
    s1 = chip.place(s_at + n0, H_MLA, T)
    pt = chip.place(pt_at, n0 + n1)
    stats = chip.small[:, 0:32]
    scale = float(D_QK) ** -0.5
    with stage(chip, "scores_ready", "shifted", "exps_ready", "probs_ready", "turned_ready", "turned_copied",
               "out_ready", "dve_chain") as \
            (block, scores_ready, shifted, exps_ready, probs_ready, turned_ready, turned_copied,
             out_ready, dve_chain):
        ps0 = chip.psum[:, 0:n0].rearrange("p (h s) -> p h s", s=P)
        ps1 = chip.psum[:, n0:n0 + n1].rearrange("p (h s) -> p h s", s=T)
        mask = over(chip.con("causal_add"), H_MLA)

        @block.tensor
        def _(pe):
            for hd in range(H_MLA):
                pe.matmul(ps0[:, hd, :], q[:, hd, 0:P], k[:, hd, 0:P], start=True, stop=True)
            for hd in range(H_MLA):
                ins = pe.matmul(ps1[:, hd, :], q[:, hd, P:T], k[:, hd, :], start=True, stop=True)
            ins.then_inc(scores_ready, 1)
            pe.wait_ge(probs_ready, 2)
            ident = chip.con("ident")
            for hd in range(H_MLA):
                pe.transpose(ps0[:, hd, :], s0[:, hd, :], ident)
            for hd in range(H_MLA):
                for b in range(NT):
                    ins = pe.transpose(ps1[:, hd, b * P:(b + 1) * P], s1[:, hd, b * P:(b + 1) * P], ident)
            ins.then_inc(turned_ready, 1)
            pe.wait_ge(turned_copied, 2)
            for hd in range(H_MLA):
                rows = slice((hd % 2) * D_V, (hd % 2 + 1) * D_V)
                out = chip.psum[rows, 6 * BANK + (hd // 2) * T:6 * BANK + (hd // 2 + 1) * T]
                vh = slice(hd * D_V, (hd + 1) * D_V)
                pe.matmul(out[:, 0:P], v[:, 0, vh], pt[:, hd * P:(hd + 1) * P], start=True, stop=True)
                for b in range(NT):
                    at = n0 + hd * T + b * P
                    ins = pe.matmul(out[:, P:T], v[:, b, vh], pt[:, at:at + P], start=(b == 0), stop=(b == NT - 1))
            ins.then_inc(out_ready, 1)

        @block.vector
        def _(dve):
            chain = Chain(dve, dve_chain)
            dve.wait_ge(scores_ready, 1)
            dve.scalar_tensor_tensor(s0, ps0, scale, mask, ALU.mult, ALU.add)
            dve.tensor_scalar(s1[:, :, 0:P], ps1[:, :, 0:P], scale, None, ALU.mult)
            chain(dve.scalar_tensor_tensor(s1[:, :, P:T], ps1[:, :, P:T], scale, mask, ALU.mult, ALU.add))
            for b, s in ((0, s0), (1, s1)):
                top = stats[:, b * 8:b * 8 + 8]
                chain(dve.tensor_reduce(top, s, AX.X, ALU.max))
                chain(dve.tensor_tensor(s, s, spread(top, s.shape[2]), ALU.subtract), shifted)
            for b, s in ((0, s0), (1, s1)):
                total = stats[:, 16 + b * 8:24 + b * 8]
                dve.wait_ge(exps_ready, b + 1)
                chain(dve.tensor_reduce(total, s, AX.X, ALU.add))
                chain(dve.reciprocal(total, total))
                dve.tensor_tensor(s, s, spread(total, s.shape[2]), ALU.mult).then_inc(probs_ready, 1)
            dve.wait_ge(turned_ready, 1)
            dve.tensor_copy(pt[:, 0:1536], chip.psum[:, 0:1536]).then_inc(turned_copied, 1)
            dve.wait_ge(out_ready, 1)
            dve.tensor_copy(o, chip.psum[:, 6 * BANK:8 * BANK].rearrange("p (h t) -> p h t", t=T))

        @block.scalar
        def _(act):
            for b, s in ((0, s0), (1, s1)):
                act.wait_ge(shifted, b + 1)
                act.activation(s, s, ACT.Exp).then_inc(exps_ready, 1)
            act.wait_ge(turned_ready, 1)
            act.activation(pt[:, 1536:3072], chip.psum[:, 1536:3072], ACT.Identity).then_inc(turned_copied, 1)

    oa = chip.place(OA, KD, T)
    project(chip, ("mla_o", l), lambda i, k: o[:, k, :], 4, store_with_act(lambda i: oa[:, i, :]))


def sigmoid_steps(chain, dve, ap):
    chain(dve.tensor_scalar(ap, ap, 1.0, None, ALU.add))
    chain(dve.reciprocal(ap, ap))


def rwkv_branch(chip, l):
    h = chip.place(H0, KD, T)
    slot = lambda i, *dims, rows=D_RW: chip.place(WORK + 1024 * i, *(dims or (H_RW, T)), rows=rows)
    raw = chip.place(WORK, 3 * H_RW + 2, T + 1, rows=D_RW)
    raw_g = chip.place(OC, T + 1)
    raw_v = chip.place(OC + 260, T + 1, rows=R_MV)
    mixed = chip.place(WORK + 4096, 3 * H_RW + 2, T, rows=D_RW)
    r, k, v = mixed[:, 0:4, :], mixed[:, 4:8, :], mixed[:, 8:12, :]
    xw, xa = mixed[:, 12, :], mixed[:, 13, :]
    xg, xv = chip.place(OC + 520, T), chip.place(OC + 780, T, rows=R_MV)
    col = lambda name: chip.col((name, l), 0, H_RW, D_RW)
    v_first = chip.place(V_FIRST, H_RW, T, rows=D_RW)

    def raw_tile(i):
        return raw[:, i, 1:T + 1] if i < 3 * H_RW + 2 else raw_g[:, 1:T + 1]
    project(chip, ("rwkv_in", l), lambda i, k: h[:, k, :], KD, store_with_act(raw_tile))
    if l:
        project(chip, ("v1", l), lambda i, k: h[:, k, :], KD, store_with_act(lambda i: raw_v[:, 1:T + 1]))

    with stage(chip, "dve_chain") as (block, dve_chain):
        @block.vector
        def _(dve):
            chain = Chain(dve, dve_chain)
            dve.memset(raw[:, :, 0:1], 0.0)
            dve.memset(raw_v[:, 0:1], 0.0)
            chain(dve.memset(raw_g[:, 0:1], 0.0))
            chain(dve.tensor_tensor(mixed, raw[:, :, 0:T], raw[:, :, 1:T + 1], ALU.subtract))
            for j in range(3 * H_RW + 2):
                chain(dve.scalar_tensor_tensor(mixed[:, j, :], mixed[:, j, :], chip.col(("mu", l), j, rows=D_RW),
                                               raw[:, j, 1:T + 1], ALU.mult, ALU.add))
            series = [(xg, raw_g, chip.col(("mu_g", l)))]
            if l:
                series.append((xv, raw_v, chip.col(("v_mu", l), rows=R_MV)))
            for x, raw_x, mu in series:
                chain(dve.tensor_tensor(x, raw_x[:, 0:T], raw_x[:, 1:T + 1], ALU.subtract))
                chain(dve.scalar_tensor_tensor(x, x, mu, raw_x[:, 1:T + 1], ALU.mult, ALU.add))

    log_w, a, g, share = slot(8), slot(10), slot(13), slot(15)
    groups = [("w2", xw), ("a2", xa)] + [("v2", xv)] * (l > 0) + [("g2", xg)]
    products = {name: chip.psum[0:D_RW, 1024 * n:1024 * (n + 1)].rearrange("p (h t) -> p h t", t=T)
                for n, (name, _) in enumerate(groups)}
    gated = [("w2", log_w, "w0"), ("a2", a, "a0")] + [("v2", share, "v0")] * (l > 0)
    with stage(chip, "inputs_ready", "gate_ready", "products_ready", "sums_ready", "sigmoids_ready",
               "dve_chain") as \
            (block, inputs_ready, gate_ready, products_ready, sums_ready, sigmoids_ready, dve_chain):

        @block.sync
        def _(sp):
            for n, (name, _) in enumerate(groups):
                blocks = chip.groups[name, l]
                for b in blocks:
                    if b.ends_unit and b.unit + RING < chip.n_units:
                        sp.wait_ge(products_ready, n + 1)
                        chip.load_unit(sp, b.unit + RING)

        @block.scalar
        def _(act):
            act.activation(xw, xw, ACT.Tanh).then_inc(inputs_ready, 1)
            act.activation(xg, xg, ACT.Sigmoid).then_inc(gate_ready, 1)
            for n, (name, dst, _) in enumerate(gated):
                act.wait_ge(sums_ready, n + 1)
                act.activation(dst, dst, ACT.Sigmoid).then_inc(sigmoids_ready, 1)

        @block.tensor
        def _(pe):
            pe.wait_ge(inputs_ready, 1)
            for name, x in groups:
                if name == "g2":
                    pe.wait_ge(gate_ready, 1)
                blocks = chip.groups[name, l]
                for hd in range(H_RW):
                    chip.arrived(pe, blocks, hd)
                    ins = pe.matmul(products[name][:, hd, :], chip.weight(blocks[hd]), x, start=True, stop=True)
                ins.then_inc(products_ready, 1)

        @block.vector
        def _(dve):
            chain = Chain(dve, dve_chain)
            for n, (name, dst, bias) in enumerate(gated):
                dve.wait_ge(products_ready, n + 1)
                dve.tensor_tensor(dst, products[name], spread(col(bias), T), ALU.add).then_inc(sums_ready, 1)
            dve.wait_ge(products_ready, len(groups))
            dve.tensor_copy(g, products["g2"])
            dve.wait_ge(sigmoids_ready, len(gated))
            chain(dve.tensor_scalar(log_w, log_w, -float(np.exp(-0.5)), None, ALU.mult))
            if l:
                chain(dve.tensor_tensor(slot(14), v_first, v, ALU.subtract))
                chain(dve.tensor_tensor(slot(14), slot(14), share, ALU.mult))
                dve.tensor_tensor(v, v, slot(14), ALU.add)
            else:
                dve.tensor_copy(v_first, v)

    total, kk, k2, tmp, tmp2, bonus = slot(9), slot(11), slot(12), slot(14), slot(15), slot(16)
    restart = slot(0)
    r_t, k_t, a_t, b_t = slot(1), slot(2), slot(3), slot(14)
    flat = lambda ap: ap.rearrange("p h t -> p (h t)")
    by_chunk = lambda ap: ap.rearrange("p h (c t) -> p (h c) t", t=P)
    ones = chip.con("ones", D_RW, D_RW)
    factor = chip.small[0:D_RW, 32:36]
    with stage(chip, "squares_ready", "products_ready", "norms_summed", "bonus_summed", "roots_ready",
               "exponents_ready", "exps_ready", "dve_chain") as \
            (block, squares_ready, products_ready, norms_summed, bonus_summed, roots_ready,
             exponents_ready, exps_ready, dve_chain):
        psn, psb = chip.psum[0:D_RW, 0:1024], chip.psum[0:D_RW, 1024:2048]

        @block.tensor
        def _(pe):
            for src, dst, need, done in ((tmp, psn, squares_ready, norms_summed),
                                         (tmp2, psb, products_ready, bonus_summed)):
                pe.wait_ge(need, 1)
                for n in range(2):
                    sl = slice(n * BANK, (n + 1) * BANK)
                    ins = pe.matmul(dst[:, sl], ones, flat(src)[:, sl], start=True, stop=True)
                ins.then_inc(done, 1)

        @block.scalar
        def _(act):
            act.wait_ge(norms_summed, 1)
            act.activation(flat(tmp), psn, ACT.Sqrt).then_inc(roots_ready, 1)
            act.wait_ge(exponents_ready, 1)
            act.activation(r_t, total, ACT.Exp)
            act.activation(k_t, total, ACT.Exp, scale=-1.0)
            act.activation(a_t, a_t, ACT.Exp)
            act.activation(factor, factor, ACT.Exp).then_inc(exps_ready, 1)

        @block.vector
        def _(dve):
            chain = Chain(dve, dve_chain)
            chain(dve.tensor_tensor(kk, k, spread(col("k_k"), T), ALU.mult))
            dve.tensor_tensor(tmp, kk, kk, ALU.mult).then_inc(squares_ready, 1)
            chain(dve.tensor_scalar(k2, a, -1.0, None, ALU.add))
            chain(dve.tensor_tensor(k2, k2, spread(col("k_a"), T), ALU.mult))
            chain(dve.scalar_tensor_tensor(k2, k2, 1.0, k, ALU.add, ALU.mult))
            chain(dve.tensor_tensor(tmp2, r, k2, ALU.mult))
            dve.wait_ge(squares_ready, 1)
            dve.tensor_tensor(tmp2, tmp2, spread(col("r_k"), T), ALU.mult).then_inc(products_ready, 1)
            chain(dve.memset(restart, 1.0))
            chain(dve.memset(by_chunk(restart)[:, :, 0:1], 0.0))
            chain(dve.tensor_tensor_scan(flat(total), flat(restart), flat(log_w), 0.0, ALU.mult, ALU.add))
            halves = total.rearrange("p h (c t) -> p h c t", t=P)
            mid = P // 2 - 1
            chain(dve.tensor_tensor(factor, halves[:, :, 0, P - 1], halves[:, :, 0, mid], ALU.subtract))
            chain(dve.tensor_tensor(factor, factor, halves[:, :, 1, mid], ALU.add))
            ref = chip.small[0:D_RW, 40:48]
            chain(dve.tensor_copy(ref, by_chunk(total)[:, :, mid]))
            chain(dve.tensor_tensor(by_chunk(total), by_chunk(total), spread(ref, P), ALU.subtract))
            dve.tensor_tensor(a_t, total, log_w, ALU.subtract).then_inc(exponents_ready, 1)
            dve.wait_ge(roots_ready, 1)
            chain(dve.tensor_scalar(tmp, tmp, 1e-12, None, ALU.max))
            chain(dve.reciprocal(tmp, tmp))
            chain(dve.tensor_tensor(kk, kk, tmp, ALU.mult))
            dve.wait_ge(bonus_summed, 1)
            dve.tensor_tensor(bonus, psb.rearrange("p (h t) -> p h t", t=T), v, ALU.mult)
            dve.wait_ge(exps_ready, 1)
            dve.tensor_tensor(r_t, r_t, r, ALU.mult)
            dve.scalar_tensor_tensor(a_t, a_t, -1.0, kk, ALU.mult, ALU.mult)
            chain(dve.tensor_tensor(b_t, kk, a, ALU.mult))
            chain(dve.tensor_tensor(b_t, b_t, k_t, ALU.mult))
            dve.tensor_tensor(k_t, k_t, k2, ALU.mult)

    N = H_RW * NT
    square = lambda i: slot(i, N, P, rows=P)
    ab, ak, rb, rk = square(4), square(5), square(8), square(9)
    inv, inv_t, half, below = square(10), square(11), square(12), square(15)
    v_tok = chip.place(WORK, N, D_RW)
    b_tok = chip.place(WORK + 512, N, D_RW)
    k_tok = chip.place(WORK + 7 * 1024, N, D_RW)
    work = chip.place(WORK + 7 * 1024 + 512, H_RW, D_RW)
    state = chip.place(WORK + 7 * 1024 + 768, H_RW, D_RW, rows=D_RW)
    pairs = lambda at: chip.psum[:, at:at + 1024].rearrange("p (j t) -> p j t", t=P)
    with stage(chip, "products_ready", "products_taken", "turned_ready") as (block, ready, taken, turned_ready):
        todo = [(ab, b_t, a_t, "strict"), (ak, k_t, a_t, "strict"), (rb, b_t, r_t, "incl"), (rk, k_t, r_t, "incl")]

        @block.tensor
        def _(pe):
            for n, (_, left, right, _) in enumerate(todo):
                for j in range(N):
                    ins = pe.matmul(pairs(1024 * n)[:, j, :], by_chunk(left)[:, j, :], by_chunk(right)[:, j, :],
                                    start=True, stop=True)
                ins.then_inc(ready, 1)
            for n, src in enumerate((v, b_t, k_t)):
                pe.wait_ge(taken, n // 2 + 1)
                for j in range(N):
                    ins = pe.transpose(chip.bank(n)[:, j * D_RW:(j + 1) * D_RW], by_chunk(src)[:, j, :],
                                       chip.con("ident", D_RW, D_RW))
            ins.then_inc(turned_ready, 1)

        @block.vector
        def _(dve):
            for n, (dst, _, _, mask) in enumerate(todo):
                dve.wait_ge(ready, n + 1)
                dve.tensor_tensor(dst, pairs(1024 * n), over(chip.con(mask, cols=P), N), ALU.mult).then_inc(taken, 1)
            dve.tensor_copy(inv, over(chip.con("ident"), N))
            dve.tensor_copy(inv_t, over(chip.con("ident"), N))
            dve.wait_ge(turned_ready, 1)
            for n, dst in enumerate((v_tok, b_tok, k_tok)):
                dve.tensor_copy(dst, chip.bank(n).rearrange("p (j e) -> p j e", e=D_RW))

    with stage(chip, "below_ready", "half_ready", "half_copied", "terms_ready", "inverse_ready", "dve_chain") as \
            (block, below_ready, half_ready, half_copied, terms_ready, inverse_ready, dve_chain):

        @block.tensor
        def _(pe):
            for n in range(N_LEVELS):
                pe.wait_ge(below_ready, n + 1)
                if n:
                    pe.wait_ge(inverse_ready, n)
                for j in range(N):
                    ins = pe.matmul(pairs(0)[:, j, :], below[:, j, :], inv[:, j, :], start=True, stop=True)
                ins.then_inc(half_ready, 1)
                pe.wait_ge(half_copied, n + 1)
                for j in range(N):
                    pe.matmul(pairs(1024)[:, j, :], inv_t[:, j, :], half[:, j, :], start=True, stop=True)
                for j in range(N):
                    ins = pe.matmul(pairs(2048)[:, j, :], half[:, j, :], inv_t[:, j, :], start=True, stop=True)
                ins.then_inc(terms_ready, 1)

        @block.vector
        def _(dve):
            for n in range(N_LEVELS):
                dve.tensor_tensor(below, ab, over(chip.con(("level", n)), N), ALU.mult).then_inc(below_ready, 1)
                dve.wait_ge(half_ready, n + 1)
                dve.tensor_copy(half, pairs(0)).then_inc(half_copied, 1)
                dve.wait_ge(terms_ready, n + 1)
                dve.tensor_tensor(inv, inv, pairs(1024), ALU.add)
                dve.tensor_tensor(inv_t, inv_t, pairs(2048), ALU.add).then_inc(inverse_ready, 1)

    y = slot(6)
    sa = chip.place(WORK + 4 * 1024, H_RW, D_RW)
    with stage(chip, "rhs_ready", "rhs_copied", "sa_ready", "sa_copied", "out_ready", "state_ready", "state_scaled") as \
            (block, rhs_ready, rhs_copied, sa_ready, sa_copied, out_ready, state_ready, state_scaled):
        rhs_ps = chip.bank(0, 256).rearrange("p (h e) -> p h e", e=D_RW)
        sa_ps = chip.bank(1, 256).rearrange("p (h e) -> p h e", e=D_RW)
        state_ps = chip.bank(2, 256, rows=D_RW).rearrange("p (h e) -> p h e", e=D_RW)
        y_ps = chip.psum[0:D_RW, 1536:2560].rearrange("p (h t) -> p h t", t=T)

        @block.tensor
        def _(pe):
            for c in range(NT):
                if c:
                    pe.wait_ge(state_scaled, 1)
                for hd in range(H_RW):
                    j = hd * NT + c
                    ins = pe.matmul(rhs_ps[:, hd, :], ak[:, j, :], v_tok[:, j, :], start=True, stop=(c == 0))
                    if c:
                        ins = pe.matmul(rhs_ps[:, hd, :], by_chunk(a_t)[:, j, :], state[:, hd, :], start=False, stop=True)
                ins.then_inc(rhs_ready, 1)
                pe.wait_ge(rhs_copied, c + 1)
                for hd in range(H_RW):
                    ins = pe.matmul(sa_ps[:, hd, :], inv_t[:, hd * NT + c, :], work[:, hd, :], start=True, stop=True)
                ins.then_inc(sa_ready, 1)
                pe.wait_ge(sa_copied, c + 1)
                if c == 0:
                    for hd in range(H_RW):
                        pe.matmul(state_ps[:, hd, :], b_tok[:, hd * NT, :], sa[:, hd, :], start=True, stop=False)
                        ins = pe.matmul(state_ps[:, hd, :], k_tok[:, hd * NT, :], v_tok[:, hd * NT, :],
                                        start=False, stop=True)
                    ins.then_inc(state_ready, 1)
                for hd in range(H_RW):
                    j = hd * NT + c
                    out = y_ps[:, hd, c * P:(c + 1) * P]
                    pe.matmul(out, sa[:, hd, :], rb[:, j, :], start=True, stop=False)
                    ins = pe.matmul(out, v_tok[:, j, :], rk[:, j, :], start=False, stop=(c == 0))
                    if c:
                        ins = pe.matmul(out, state[:, hd, :], by_chunk(r_t)[:, j, :], start=False, stop=True)
                ins.then_inc(out_ready, 1)

        @block.vector
        def _(dve):
            for c in range(NT):
                dve.wait_ge(rhs_ready, c + 1)
                dve.tensor_copy(work, rhs_ps).then_inc(rhs_copied, 1)
                dve.wait_ge(sa_ready, c + 1)
                if c:
                    dve.wait_ge(out_ready, c)
                dve.tensor_copy(sa, sa_ps).then_inc(sa_copied, 1)
                if c == 0:
                    dve.wait_ge(state_ready, 1)
                    dve.tensor_tensor(state, state_ps, spread(factor, D_RW), ALU.mult).then_inc(state_scaled, 1)
            dve.wait_ge(out_ready, NT)
            dve.tensor_copy(y, y_ps)

    norm(chip, y, y, slot(4), H_RW, 1, D_RW, GN_EPS, gain=lambda j: chip.col(("ln_w", l), j, rows=D_RW),
         bias=lambda j: chip.col(("ln_b", l), j, rows=D_RW), center=True)
    with stage(chip, "dve_chain") as (block, dve_chain):
        @block.vector
        def _(dve):
            chain = Chain(dve, dve_chain)
            chain(dve.tensor_tensor(y, y, bonus, ALU.add))
            dve.tensor_tensor(y, y, g, ALU.mult)
    ob = chip.place(OB, KD, T)
    project(chip, ("rwkv_o", l), lambda i, k: y[:, k, :], H_RW, store_with_act(lambda i: ob[:, i, :]))


def conv_branch(chip, l):
    h, oc = chip.place(H0, KD, T), chip.place(OC, KD, T)
    parts = chip.place(WORK, 6, T)
    u = chip.place(WORK + 6 * T, 2, T + 2)
    y = chip.place(WORK + 6 * T + 2 * (T + 2), 2, T)
    project(chip, ("conv_in", l), lambda i, k: h[:, k, :], KD, store_with_act(lambda i: parts[:, i, :]))
    with stage(chip, "dve_chain") as (block, dve_chain):
        @block.vector
        def _(dve):
            chain = Chain(dve, dve_chain)
            dve.memset(u[:, :, 0:2], 0.0)
            chain(dve.tensor_tensor(u[:, :, 2:T + 2], parts[:, 2:4, :], parts[:, 4:6, :], ALU.mult))
            for j in range(2):
                tap = lambda n: chip.col(("conv_w", l), 2 * n + j)
                chain(dve.tensor_scalar(y[:, j, :], u[:, j, 2:T + 2], tap(2), None, ALU.mult))
                for n in (1, 0):
                    chain(dve.scalar_tensor_tensor(y[:, j, :], u[:, j, n:n + T], tap(n), y[:, j, :],
                                                   ALU.mult, ALU.add))
            dve.tensor_tensor(y, y, parts[:, 0:2, :], ALU.mult)
    project(chip, ("conv_o", l), lambda i, k: y[:, k, :], 2, store_with_act(lambda i: oc[:, i, :]))


def merge_branches(chip, l):
    h, merged = chip.place(H0, KD, T), chip.place(WORK, KD, T)
    o = chip.place(OA, 3, KD * T)
    e = [chip.place(WORK + 2048 + 768 * b, 3, T) for b in range(2)]

    def gates(block, s, banks, steps):
        @block.scalar
        def _(act):
            for i in range(steps):
                act.wait_ge(s["ready"], i + 1)
                if i >= 2:
                    act.wait_ge(s["dve_done"], i - 1)
                base = (i % 2) * 3 * BANK
                psum = chip.psum[:, base:base + 3 * BANK].rearrange("p (j t) -> p j t", t=BANK)[:, :, 0:T]
                act.activation(e[i % 2], psum, ACT.Sigmoid).then_inc(s["free"], 1)

        @block.vector
        def _(dve):
            chain = Chain(dve, s["dve_chain"])
            for i in range(steps):
                t = e[i % 2]
                dve.wait_ge(s["free"], i + 1)
                chain(dve.tensor_tensor(t, t, o[:, :, i * T:(i + 1) * T], ALU.mult))
                chain(dve.tensor_tensor(t[:, 0, :], t[:, 0, :], t[:, 1, :], ALU.add))
                dve.tensor_tensor(merged[:, i, :], t[:, 0, :], t[:, 2, :], ALU.add).then_inc(s["dve_done"], 1)

    project(chip, ("gates", l), lambda i, k: h[:, k, :], KD, gates, per=3)
    project(chip, ("w_out", l), lambda i, k: merged[:, k, :], KD, add_to_x(chip))


def add_to_x(chip):
    x = chip.x[:, :].rearrange("p (c t) -> p c t", t=T)

    def epilogue(block, s, banks, steps):
        @block.vector
        def _(dve):
            for i in range(steps):
                s["side_work"](dve, i)
                dve.wait_ge(s["ready"], i + 1)
                dve.tensor_tensor(x[:, i, :], x[:, i, :], banks(i)[0], ALU.add).then_inc(s["free"], 1)
    return epilogue


def first_layer(chip, l):
    x = chip.x[:, :].rearrange("p (c t) -> p c t", t=T)
    h = chip.place(H0, KD, T)
    norm(chip, x, h, chip.place(WORK, KD, T), 1, KD, P, RMS_EPS, gain=lambda k: chip.col(("attn_norm", l), k))
    mla_branch(chip, l)
    rwkv_branch(chip, l)
    conv_branch(chip, l)
    merge_branches(chip, l)
    norm(chip, x, h, chip.place(WORK, KD, T), 1, KD, P, RMS_EPS, gain=lambda k: chip.col(("mlp_norm", l), k))
    inner = chip.place(WORK, F1 // P, T)
    relu = [chip.stat[:, b * T:(b + 1) * T] for b in range(2)]

    def squared_relu(block, s, banks, steps):
        @block.scalar
        def _(act):
            chain = Chain(act, s["act_chain"])
            for i in range(steps):
                act.wait_ge(s["ready"], i + 1)
                chain(act.activation(relu[i % 2], banks(i)[0], ACT.Relu), s["free"])
                act.activation(inner[:, i, :], relu[i % 2], ACT.Square)

        @block.vector
        def _(dve):
            for i in range(steps):
                s["side_work"](dve, i)

    project(chip, ("up", l), lambda i, k: h[:, k, :], KD, squared_relu)
    project(chip, ("down", l), lambda i, k: inner[:, k, :], F1 // P, add_to_x(chip))



LAYERS = list(range(L2))
SLOT = KD * T


def slot2(chip, i, *dims, at=0, rows=P):
    return chip.place(SLOT * i + at, *(dims or (KD, T)), rows=rows)


def prepare_conditioning(chip):
    logits = chip.col("lb", 0, L2 * KD).rearrange("p (l c) -> p l c", c=KD)
    shares = chip.small[:, 72:104].rearrange("p (l c) -> p l c", c=KD)
    top = chip.small[:, 104:112]
    with stage(chip, "dve_chain", "shifted", "exps_ready") as (block, dve_chain, shifted, exps_ready):

        @block.scalar
        def _(act):
            act.activation(chip.silu_c, chip.col("c", 0, KD), ACT.Silu)
            act.wait_ge(shifted, 1)
            act.activation(shares, shares, ACT.Exp).then_inc(exps_ready, 1)

        @block.vector
        def _(dve):
            chain = Chain(dve, dve_chain)
            chain(dve.tensor_tensor(top, logits[:, 0, :], logits[:, 1, :], ALU.max))
            for l in range(2, L2):
                chain(dve.tensor_tensor(top, top, logits[:, l, :], ALU.max))
            dve.tensor_tensor(shares, logits, over(top, L2), ALU.subtract).then_inc(shifted, 1)
            dve.wait_ge(exps_ready, 1)
            chain(dve.tensor_tensor(top, shares[:, 0, :], shares[:, 1, :], ALU.add))
            for l in range(2, L2):
                chain(dve.tensor_tensor(top, top, shares[:, l, :], ALU.add))
            chain(dve.reciprocal(top, top))
            chain(dve.tensor_tensor(chip.lb, shares[:, 1, :], top, ALU.mult))
            dve.tensor_scalar(chip.lb_rest, chip.lb, -1.0, 1.0, ALU.mult, ALU.add)


def finish_conditioning(chip, layers):
    n_out = 6 * KD
    with stage(chip, "sums_ready", "dve_chain") as (block, sums_ready, dve_chain):

        @block.tensor
        def _(pe):
            for j, i in enumerate(layers):
                for m in range(n_out):
                    ins = pe.matmul(chip.bank(j, 1, at=m), chip.ada_sums[i % 2][:, m * P:(m + 1) * P],
                                    chip.con("ones", cols=1), start=True, stop=True)
                ins.then_inc(sums_ready, 1)

        @block.vector
        def _(dve):
            chain = Chain(dve, dve_chain)
            for j, i in enumerate(layers):
                to = chip.ada[:, i * n_out:(i + 1) * n_out]
                dve.wait_ge(sums_ready, j + 1)
                chain(dve.tensor_tensor(to, chip.bank(j, n_out), chip.col(("ada_b", i), 0, n_out), ALU.add))
                for half in range(2):
                    at = (3 * half + 1) * KD
                    chain(dve.tensor_scalar(to[:, at:at + 2 * KD], to[:, at:at + 2 * KD], 1.0, None, ALU.add))


def ada_col(chip, i, which, k):
    at = (i * 6 + which) * KD + k
    return chip.ada[:, at:at + 1]


def modulate(chip, i, j):
    x = chip.x[:, :].rearrange("p (c t) -> p c t", t=T)
    h = slot2(chip, 0)
    with stage(chip) as (block,):
        @block.scalar
        def _(act):
            for k in range(0, KD, 2):
                act.activation(h[:, k, :], x[:, k, :], ACT.Identity, scale=ada_col(chip, i, 3 * j + 1, k),
                               bias=ada_col(chip, i, 3 * j, k))

        @block.vector
        def _(dve):
            for k in range(1, KD, 2):
                dve.tensor_scalar(h[:, k, :], x[:, k, :], ada_col(chip, i, 3 * j + 1, k),
                                  ada_col(chip, i, 3 * j, k), ALU.mult, ALU.add)


def residual(chip, i, j, bias=None):
    x = chip.x[:, :].rearrange("p (c t) -> p c t", t=T)
    gated = [chip.stat[:, b * T:(b + 1) * T] for b in range(4)]

    def epilogue(block, s, banks, steps):
        @block.vector
        def _(dve):
            chain = Chain(dve, s["dve_chain"])
            for n in range(steps):
                gate = ada_col(chip, i, 3 * j + 2, n)
                dve.wait_ge(s["ready"], n + 1)
                if bias:
                    ins = dve.tensor_scalar(gated[n % 4], banks(n)[0], bias(n), gate, ALU.add, ALU.mult)
                else:
                    ins = dve.tensor_scalar(gated[n % 4], banks(n)[0], gate, None, ALU.mult)
                ins.then_inc(s["free"], 1)
                dve.wait_ge(s["free"], n + 1)
                dve.scalar_tensor_tensor(x[:, n, :], x[:, n, :], ALPHA, gated[n % 4], ALU.mult, ALU.add)
    return epilogue


def post_norm(chip, i, j):
    x = chip.x[:, :].rearrange("p (c t) -> p c t", t=T)
    norm(chip, x, x, slot2(chip, 1), 1, KD, P, LN_EPS, gain=lambda k: chip.col(("post_g", i, j), k),
         bias=lambda k: chip.col(("post_b", i, j), k), center=True)


def silu_into(dst, buffers=None, times=None):
    def epilogue(block, s, banks, steps):
        @block.scalar
        def _(act):
            for i in range(steps):
                act.wait_ge(s["ready"], i + 1)
                if times and i >= 2:
                    act.wait_ge(s["dve_done"], i - 1)
                act.activation(buffers[i % 2] if times else dst(i), banks(i)[0], ACT.Silu).then_inc(s["free"], 1)

        @block.vector
        def _(dve):
            for i in range(steps if times else 0):
                dve.wait_ge(s["free"], i + 1)
                dve.tensor_tensor(dst(i), buffers[i % 2], times(i), ALU.mult).then_inc(s["dve_done"], 1)
    return epilogue


def conv_ffn(chip, i):
    h = slot2(chip, 0)
    inner = chip.place(SLOT, KF, T)
    at = SLOT + KF * T
    raw = [chip.place(at + b * 2 * T, 2, T) for b in range(2)]
    conv = [chip.place(at + (2 + b) * 2 * T, 2, T) for b in range(2)]
    e = [chip.place(at + 8 * T + b * T, T) for b in range(2)]
    tap = lambda m, half, n: chip.col(("ffn_w", i), (n * 2 + half) * KF + m)

    def swiglu(block, s, banks, steps):
        @block.scalar
        def _(act):
            for m in range(steps):
                b = m % 2
                act.wait_ge(s["ready"], m + 1)
                if m >= 2:
                    act.wait_ge(s["dve_done"], 2 * m - 2)
                base = (m % 4) * 2 * BANK
                psum = chip.psum[:, base:base + 2 * BANK].rearrange("p (j t) -> p j t", t=BANK)[:, :, 0:T]
                act.activation(raw[b], psum, ACT.Identity)
                for half in range(2):
                    ins = act.activation(conv[b][:, half, :], banks(m)[half], ACT.Identity,
                                         scale=tap(m, half, 2), bias=chip.col(("ffn_b", i), half * KF + m))
                ins.then_inc(s["free"], 1)
                act.wait_ge(s["dve_done"], 2 * m + 1)
                act.activation(e[b], conv[b][:, 0, :], ACT.Silu).then_inc(s["act_done"], 1)

        @block.vector
        def _(dve):
            chain = Chain(dve, s["dve_chain"])
            for m in range(steps):
                b = m % 2
                dve.wait_ge(s["free"], m + 1)
                for half in range(2):
                    c, r = conv[b][:, half, :], raw[b][:, half, :]
                    chain(dve.scalar_tensor_tensor(c[:, 1:T], r[:, 0:T - 1], tap(m, half, 1), c[:, 1:T],
                                                   ALU.mult, ALU.add))
                    chain(dve.scalar_tensor_tensor(c[:, 2:T], r[:, 0:T - 2], tap(m, half, 0), c[:, 2:T],
                                                   ALU.mult, ALU.add), s["dve_done"] if half == 0 else None)
                dve.wait_ge(s["act_done"], m + 1)
                chain(dve.tensor_tensor(inner[:, m, :], e[b], conv[b][:, 1, :], ALU.mult), s["dve_done"])

    project(chip, ("ffn_up", i), lambda m, k: h[:, k, :], KD, swiglu, per=2)
    project(chip, ("ffn_down", i), lambda m, k: inner[:, k, :], KF, residual(chip, i, 1))


def conformer(chip, i):
    h = slot2(chip, 0)
    pad = TAPS_CC - 1
    u = chip.place(SLOT, KD, pad + T)
    conv = chip.place(3 * SLOT, KD, T)
    e = [chip.place(4 * SLOT + b * T, T) for b in range(2)]
    on_pe = 2
    diagonals = chip.place(5 * SLOT, on_pe * TAPS_CC, P)
    with stage(chip) as (block,):
        @block.vector
        def _(dve):
            dve.memset(u[:, :, 0:pad], 0.0)

        @block.scalar
        def _(act):
            for m in range(on_pe):
                for n in range(TAPS_CC):
                    act.activation(diagonals[:, m * TAPS_CC + n, :], chip.con("ident"), ACT.Identity,
                                   scale=chip.col("dw_w", n * KD + m))

    blocks = chip.groups["pw1", i]
    depth = 3
    with stage(chip, "tiles_ready", "glu_taken", "glu_ready", "conv_ready", "dve_chain") as \
            (block, ready, taken, glu_ready, conv_ready, dve_chain):

        @block.sync
        def _(sp):
            chip.refill(sp, blocks, 2 * KD, ready)

        @block.tensor
        def _(pe):
            for m in range(KD):
                if m >= depth:
                    pe.wait_ge(taken, m - depth + 1)
                for half in range(2):
                    for k in range(KD):
                        n = (2 * m + half) * KD + k
                        chip.arrived(pe, blocks, n)
                        ins = pe.matmul(chip.bank(2 * (m % depth) + half, T), chip.weight(blocks[n]), h[:, k, :],
                                        start=(k == 0), stop=(k == KD - 1))
                ins.then_inc(ready, 1)
                c = m - 2
                if 0 <= c < on_pe:
                    pe.wait_ge(glu_ready, c + 1)
                    for n in range(TAPS_CC):
                        ins = pe.matmul(chip.bank(6 + c, T), diagonals[:, c * TAPS_CC + n, :], u[:, c, n:n + T],
                                        start=(n == 0), stop=(n == TAPS_CC - 1))
                    ins.then_inc(conv_ready, 1)

        @block.scalar
        def _(act):
            for m in range(KD):
                act.wait_ge(ready, m + 1)
                if m >= 2:
                    act.wait_ge(glu_ready, m - 1)
                act.activation(u[:, m, pad:pad + T], chip.bank(2 * (m % depth), T), ACT.Identity,
                               bias=chip.col("b_pw1", m))
                act.activation(e[m % 2], chip.bank(2 * (m % depth) + 1, T), ACT.Sigmoid,
                               bias=chip.col("b_pw1", KD + m)).then_inc(taken, 1)
                c = m - 4
                if 0 <= c < on_pe:
                    act.wait_ge(conv_ready, c + 1)
                    act.activation(conv[:, c, :], chip.bank(6 + c, T), ACT.Identity, bias=chip.col("dw_b", c))

        @block.vector
        def _(dve):
            chain = Chain(dve, dve_chain)

            def glu(m):
                dve.wait_ge(taken, m + 1)
                chain(dve.tensor_tensor(u[:, m, pad:pad + T], u[:, m, pad:pad + T], e[m % 2], ALU.mult), glu_ready)

            for m in range(min(on_pe + 1, KD)):
                glu(m)
            for m in range(on_pe, KD):
                if m + 1 < KD:
                    glu(m + 1)
                for n in range(TAPS_CC):
                    w = chip.col("dw_w", n * KD + m)
                    if n == 0:
                        ins = dve.tensor_scalar(conv[:, m, :], u[:, m, 0:T], w, chip.col("dw_b", m), ALU.mult, ALU.add)
                    else:
                        ins = dve.scalar_tensor_tensor(conv[:, m, :], u[:, m, n:n + T], w, conv[:, m, :],
                                                       ALU.mult, ALU.add)
                    chain(ins)

    norm(chip, conv, conv, slot2(chip, 4), 1, KD, P, LN_EPS, gain=lambda k: chip.col("cc_g", k),
         bias=lambda k: chip.col("cc_b", k), center=True)
    with stage(chip) as (block,):
        @block.scalar
        def _(act):
            act.activation(conv, conv, ACT.Silu)
    project(chip, ("pw2", i), lambda m, k: conv[:, k, :], KD,
            residual(chip, i, 0, bias=lambda m: chip.col("b_pw2", m)))


def hgrn(chip, i):
    h = slot2(chip, 0)
    q, f, k, v, g = (slot2(chip, n) for n in range(1, 6))
    v = chip.place(4 * SLOT, NT, D)
    b_sum, t1, t2, qe, ke = (slot2(chip, n) for n in (6, 7, 8, 9, 10))
    e = [chip.place(8 * SLOT + n * T, T) for n in range(2)]
    n_chunks, per_tile = T // C_HG, P // C_HG
    project(chip, ("hg_q", i), lambda m, k: h[:, k, :], KD, silu_into(lambda m: q[:, m, :]))

    def forget(block, s, banks, steps):
        @block.scalar
        def _(act):
            for m in range(steps):
                act.wait_ge(s["ready"], m + 1)
                if m >= 2:
                    act.wait_ge(s["dve_done"], m - 1)
                act.activation(e[m % 2], banks(m)[0], ACT.Sigmoid).then_inc(s["free"], 1)

        @block.vector
        def _(dve):
            chain = Chain(dve, s["dve_chain"])
            for m in range(steps):
                dve.wait_ge(s["free"], m + 1)
                chain(dve.tensor_scalar(f[:, m, :], e[m % 2], chip.lb_rest[:, m:m + 1], chip.lb[:, m:m + 1],
                                        ALU.mult, ALU.add), s["dve_done"])
                dve.tensor_scalar(k[:, m, :], f[:, m, :], -1.0, 1.0, ALU.mult, ALU.add)

    project(chip, ("hg_f", i), lambda m, k: h[:, k, :], KD, forget)
    project_tokens(chip, ("hg_v", i), lambda k: h[:, k, :], KD, lambda tt, n: v[:, tt, n * BANK:(n + 1) * BANK])
    project(chip, ("hg_g", i), lambda m, k: h[:, k, :], KD, silu_into(lambda m: g[:, m, :]))

    flat = lambda ap: ap.rearrange("p c t -> p (c t)")
    chunks = lambda ap: ap.rearrange("p c (n t) -> p (c n) t", t=C_HG)
    decay = chip.small[:, 64:128]
    with stage(chip, "logs_ready", "exponents_ready", "exps_ready", "factors_used", "dve_chain") as \
            (block, logs_ready, exponents_ready, exps_ready, factors_used, dve_chain):
        @block.scalar
        def _(act):
            act.activation(f, f, ACT.Ln).then_inc(logs_ready, 1)
            act.wait_ge(exponents_ready, 1)
            act.activation(qe, t1, ACT.Exp)
            act.activation(ke, t1, ACT.Exp, scale=-1.0).then_inc(exps_ready, 1)
            act.activation(f, b_sum, ACT.Exp).then_inc(exps_ready, 1)
            act.wait_ge(exponents_ready, 2)
            act.activation(t2, t2, ACT.Exp).then_inc(exps_ready, 1)
            act.activation(decay, chunks(b_sum)[:, :, C_HG - 1], ACT.Exp)

        @block.vector
        def _(dve):
            chain = Chain(dve, dve_chain)
            chain(dve.memset(t2, 1.0))
            chain(dve.memset(chunks(t2)[:, :, 0:1], 0.0))
            dve.wait_ge(logs_ready, 1)
            chain(dve.tensor_tensor_scan(flat(b_sum), flat(t2), flat(f), 0.0, ALU.mult, ALU.add))
            at = lambda n: chunks(b_sum)[:, :, n:n + 1].broadcast_to([P, KD * n_chunks, C_HG])
            dve.tensor_tensor(chunks(t1), chunks(b_sum), at(C_HG // 2 - 1), ALU.subtract).then_inc(exponents_ready, 1)
            dve.tensor_tensor(chunks(t2), at(C_HG - 1), chunks(b_sum), ALU.subtract).then_inc(exponents_ready, 1)
            dve.wait_ge(exps_ready, 1)
            dve.tensor_tensor(qe, qe, q, ALU.mult)
            dve.tensor_tensor(ke, ke, k, ALU.mult)
            dve.wait_ge(exps_ready, 2)
            dve.tensor_tensor(q, q, f, ALU.mult)
            dve.wait_ge(exps_ready, 3)
            dve.tensor_tensor(k, k, t2, ALU.mult)

    scores = slot2(chip, 8, 2 * H_HG, P)
    k_tok = chip.place(7 * SLOT, NT, D)
    with stage(chip, "scores_ready", "turned_ready", "dve_chain") as (block, scores_ready, turned_ready, dve_chain):
        ps = chip.psum[:, 0:2048].rearrange("p (j t) -> p j t", t=P)

        @block.tensor
        def _(pe):
            for hd in range(H_HG):
                for tt in range(NT):
                    sl = slice(tt * P, (tt + 1) * P)
                    ins = pe.matmul(ps[:, hd * NT + tt, :], ke[:, hd, sl], qe[:, hd, sl], start=True, stop=True)
            ins.then_inc(scores_ready, 1)
            for tt in range(NT):
                for hd in range(H_HG):
                    at = 2048 + tt * D + hd * P
                    ins = pe.transpose(chip.psum[:, at:at + P], k[:, hd, tt * P:(tt + 1) * P], chip.con("ident"))
            ins.then_inc(turned_ready, 1)

        @block.vector
        def _(dve):
            dve.wait_ge(scores_ready, 1)
            Chain(dve, dve_chain)(dve.tensor_scalar(scores, ps, BIG, -BIG, ALU.min, ALU.max))
            dve.tensor_tensor(scores, scores, over(chip.con("chunk"), 2 * H_HG), ALU.mult)

        @block.scalar
        def _(act):
            act.wait_ge(turned_ready, 1)
            act.activation(k_tok, chip.psum[:, 2048:4096].rearrange("p (a b) -> p a b", b=D), ACT.Identity)

    states = chip.place(9 * SLOT, H_HG, (n_chunks - 1) * P)
    with stage(chip, "updates_ready", "updates_taken", "dve_chain") as (block, ready, taken, dve_chain):
        def update(hd, n):
            pair, half = hd // 2, hd % 2
            return chip.bank(4 * (pair % 2) + n % per_tile, P, at=(half * NT + n // per_tile) * P)

        @block.tensor
        def _(pe):
            for pair in range(H_HG // 2):
                if pair >= 2:
                    pe.wait_ge(taken, pair - 1)
                for hd in (2 * pair, 2 * pair + 1):
                    for n in range(n_chunks - 1):
                        rows = slice((n % per_tile) * C_HG, (n % per_tile + 1) * C_HG)
                        ins = pe.matmul(update(hd, n), k_tok[rows, n // per_tile, hd * P:(hd + 1) * P],
                                        v[rows, n // per_tile, hd * P:(hd + 1) * P], start=True, stop=True)
                ins.then_inc(ready, 1)

        @block.vector
        def _(dve):
            chain = Chain(dve, dve_chain)
            state = lambda hd, n: states[:, hd, (n - 1) * P:n * P]
            for pair in range(H_HG // 2):
                dve.wait_ge(ready, pair + 1)
                for n in range(n_chunks - 1):
                    for hd in (2 * pair, 2 * pair + 1):
                        if n == 0:
                            ins = dve.tensor_copy(state(hd, 1), update(hd, 0))
                        else:
                            j = hd * n_chunks + n
                            ins = dve.scalar_tensor_tensor(state(hd, n + 1), state(hd, n), decay[:, j:j + 1],
                                                           update(hd, n), ALU.mult, ALU.add)
                        last = n == n_chunks - 2 and hd % 2
                        chain(ins, taken if last else None)

    o = slot2(chip, 6)
    with stage(chip, "heads_ready") as (block, heads_ready):
        @block.tensor
        def _(pe):
            for hd in range(H_HG):
                for tt in range(NT):
                    out = chip.psum[:, hd * T + tt * P:hd * T + (tt + 1) * P]
                    ins = pe.matmul(out, v[:, tt, hd * P:(hd + 1) * P], scores[:, hd * NT + tt, :],
                                    start=True, stop=False, skip_group_check=True)
                    for j in range(per_tile):
                        n = tt * per_tile + j
                        if n:
                            ins = pe.matmul(out[:, j * C_HG:(j + 1) * C_HG], states[:, hd, (n - 1) * P:n * P],
                                            q[:, hd, n * C_HG:(n + 1) * C_HG], start=False,
                                            stop=(j == per_tile - 1), skip_group_check=True)
                if hd % 2:
                    ins.then_inc(heads_ready, 1)

        @block.vector
        def _(dve):
            for pair in range(H_HG // 2):
                dve.wait_ge(heads_ready, pair + 1)
                dve.tensor_copy(o[:, 2 * pair:2 * pair + 2, :], chip.bank(pair).rearrange("p (h t) -> p h t", t=T))

    norm(chip, o, o, slot2(chip, 7), H_HG, 1, P, RMS_EPS, gain=lambda n: chip.col("hg_norm"))
    with stage(chip) as (block,):
        @block.vector
        def _(dve):
            dve.tensor_tensor(o, o, g, ALU.mult)
    project(chip, ("hg_out", i), lambda m, k: o[:, k, :], KD, residual(chip, i, 0))


def mlstm(chip, i):
    h = slot2(chip, 0)
    big = lambda n: chip.place(SLOT + 2 * SLOT * n, K_ML, T)
    xm, xc, q, k, vf = big(0), big(1), big(2), big(3), big(5)
    v = chip.place(SLOT + 2 * SLOT * 4, NT, I_ML)
    conv = [k[:, n, :] for n in range(2)]

    def convolve(block, s, banks, steps):
        @block.scalar
        def _(act):
            for m in range(steps):
                b = m % 2
                act.wait_ge(s["ready"], m + 1)
                act.activation(xm[:, m, :], banks(m)[0], ACT.Identity)
                act.activation(conv[b], banks(m)[0], ACT.Identity, scale=chip.col("ml_w", 3 * K_ML + m),
                               bias=chip.col("ml_b", m)).then_inc(s["free"], 1)
                act.wait_ge(s["dve_done"], m + 1)
                act.activation(xc[:, m, :], conv[b], ACT.Silu).then_inc(s["act_done"], 1)

        @block.vector
        def _(dve):
            chain = Chain(dve, s["dve_chain"])
            for m in range(steps):
                b = m % 2
                dve.wait_ge(s["free"], m + 1)
                for back in (1, 2, 3):
                    w = chip.col("ml_w", (3 - back) * K_ML + m)
                    chain(dve.scalar_tensor_tensor(conv[b][:, back:T], xm[:, m, 0:T - back], w, conv[b][:, back:T],
                                                   ALU.mult, ALU.add), s["dve_done"] if back == 3 else None)

    project(chip, ("ml_x", i), lambda m, k: h[:, k, :], KD, convolve)
    project(chip, ("ml_q", i), lambda m, _: xc[:, m, :], 1, store_with_act(lambda m: q[:, m, :]))
    project(chip, ("ml_k", i), lambda m, _: xc[:, m, :], 1, store_with_act(lambda m: k[:, m, :]))

    blocks = chip.groups["ml_v", i]
    with stage(chip, "tiles_ready", "features_taken", "tokens_taken") as (block, ready, features_taken, tokens_taken):
        @block.sync
        def _(sp):
            chip.refill(sp, blocks, 1, ready)

        @block.tensor
        def _(pe):
            for m in range(K_ML):
                chip.arrived(pe, blocks, m)
                if m >= 4:
                    pe.wait_ge(features_taken, m - 3)
                    pe.wait_ge(tokens_taken, m - 3)
                w = chip.weight(blocks[m])
                pe.matmul(chip.bank(m % 4, T), w, xm[:, m, :], start=True, stop=True)
                for tt in range(NT):
                    ins = pe.matmul(chip.bank(4 + m % 4, P, at=tt * P), xm[:, m, tt * P:(tt + 1) * P], w,
                                    start=True, stop=True)
                ins.then_inc(ready, 1)

        @block.scalar
        def _(act):
            for m in range(K_ML):
                act.wait_ge(ready, m + 1)
                act.activation(vf[:, m, :], chip.bank(m % 4, T), ACT.Identity).then_inc(features_taken, 1)

        @block.vector
        def _(dve):
            for m in range(K_ML):
                dve.wait_ge(ready, m + 1)
                dve.tensor_copy(v[:, :, m * P:(m + 1) * P],
                                chip.bank(4 + m % 4, T).rearrange("p (a b) -> p a b", b=P)).then_inc(tokens_taken, 1)

    row = lambda n, rows=H_ML: chip.stat[0:rows, n * T:(n + 1) * T]
    both, ig, fg, size, ln, g, ones_row, m_row = (row(n) for n in range(8))
    n_row = chip.cos[0:H_ML, :]
    g_cols = chip.small[:, 96:96 + NT * H_ML]
    spare = SLOT
    w0, w1 = chip.place(spare, H_ML, T), chip.place(spare + H_ML * T, H_ML, P)
    s0, s1 = chip.place(spare + 1536, H_ML, T), chip.place(spare + 1536 + H_ML * T, H_ML, P)
    floor = chip.place(spare + 3072, H_ML, T)
    sel = chip.con("sel")
    with stage(chip, "gates_ready", "gates_copied", "rows_ready", "size_ready", "log_ready", "series_ready",
               "spread_ready", "exponents_ready", "exps_ready", "dve_chain") as \
            (block, gates_ready, gates_copied, rows_ready, size_ready, log_ready, series_ready,
             spread_ready, exponents_ready, exps_ready, dve_chain):
        @block.tensor
        def _(pe):
            n = 0
            for src in (q, k, vf):
                for m in range(K_ML):
                    ins = pe.matmul(chip.bank(0, T, rows=2 * H_ML), chip.col("w_if", 8 * n, 8), src[:, m, :],
                                    start=(n == 0), stop=(n == 3 * K_ML - 1))
                    n += 1
            ins.then_inc(gates_ready, 1)
            pe.wait_ge(gates_copied, 1)
            for j in range(2):
                at = H_ML * P + j * H_ML
                ins = pe.matmul(chip.bank(1 + j, T, rows=H_ML), sel[0:2 * H_ML, at:at + H_ML], row(0, 2 * H_ML),
                                start=True, stop=True)
            ins.then_inc(rows_ready, 1)
            pe.wait_ge(series_ready, 1)
            for n, src in enumerate((m_row, n_row)):
                for hd in range(H_ML):
                    at = 1024 * n + hd * T
                    pe.matmul(chip.psum[:, at:at + T], sel[0:H_ML, hd * P:(hd + 1) * P], src, start=True, stop=True)
            for tt in range(NT):
                ins = pe.transpose(chip.bank(4, H_ML, at=tt * H_ML), g[:, tt * P:(tt + 1) * P],
                                   chip.con("ident", H_ML, H_ML))
            ins.then_inc(spread_ready, 1)

        @block.scalar
        def _(act):
            act.wait_ge(size_ready, 1)
            act.activation(ln, size, ACT.Exp, scale=-1.0).then_inc(exps_ready, 1)
            act.wait_ge(exps_ready, 1)
            act.activation(ln, ln, ACT.Ln, bias=1.0).then_inc(log_ready, 1)
            act.wait_ge(spread_ready, 1)
            act.activation(floor, chip.psum[:, 1024:2048].rearrange("p (h t) -> p h t", t=T), ACT.Exp, scale=-1.0)
            act.wait_ge(exponents_ready, 1)
            act.activation(w0, w0, ACT.Exp)
            act.activation(w1, w1, ACT.Exp).then_inc(exps_ready, 1)

        @block.vector
        def _(dve):
            chain = Chain(dve, dve_chain)
            dve.wait_ge(gates_ready, 1)
            dve.tensor_copy(row(0, 2 * H_ML), chip.bank(0, T, rows=2 * H_ML)).then_inc(gates_copied, 1)
            dve.memset(ones_row, 1.0)
            dve.wait_ge(rows_ready, 1)
            dve.tensor_scalar(ig, chip.bank(1, T, rows=H_ML), chip.col("b_if", 0, rows=H_ML), None, ALU.add)
            chain(dve.tensor_scalar(fg, chip.bank(2, T, rows=H_ML), chip.col("b_if", 1, rows=H_ML), None, ALU.add))
            dve.scalar_tensor_tensor(size, fg, -1.0, fg, ALU.mult, ALU.max).then_inc(size_ready, 1)
            chain(dve.tensor_scalar(fg, fg, -1.0, 0.0, ALU.mult, ALU.max))
            dve.wait_ge(log_ready, 1)
            chain(dve.scalar_tensor_tensor(fg, fg, -1.0, ln, ALU.mult, ALU.subtract))
            chain(dve.tensor_tensor_scan(size, ones_row, fg, 0.0, ALU.mult, ALU.add))
            chain(dve.tensor_tensor(g, ig, size, ALU.subtract))
            chain(dve.tensor_tensor_scan(m_row, ones_row, g, 0.0, ALU.mult, ALU.max))
            dve.tensor_tensor(n_row, size, m_row, ALU.add).then_inc(series_ready, 1)
            dve.wait_ge(spread_ready, 1)
            chain(dve.tensor_copy(g_cols, chip.bank(4, NT * H_ML)))
            m_spread = chip.psum[:, 0:1024].rearrange("p (h t) -> p h t", t=T)
            for hd in range(H_ML):
                dve.tensor_scalar(w0[:, hd, :], m_spread[:, hd, :], -1.0, g_cols[:, hd:hd + 1], ALU.mult, ALU.add)
                chain(dve.tensor_scalar(w1[:, hd, :], m_spread[:, hd, P:T], -1.0,
                                        g_cols[:, H_ML + hd:H_ML + hd + 1], ALU.mult, ALU.add))
            chain(dve.tensor_scalar(w0, w0, 0.0, None, ALU.min))
            dve.tensor_scalar(w1, w1, 0.0, None, ALU.min).then_inc(exponents_ready, 1)
            dve.wait_ge(exps_ready, 2)
            scale = float(D_ML) ** -0.5
            dve.scalar_tensor_tensor(w0, w0, scale, over(chip.con("incl", cols=T), H_ML), ALU.mult, ALU.mult)
            dve.scalar_tensor_tensor(w1, w1, scale, over(chip.con("incl", cols=P), H_ML), ALU.mult, ALU.mult)

    hc = q
    rden = chip.stat[:, 0:1024]
    per_head = D_ML // P
    with stage(chip, "scores_ready", "weighted", "sums_ready", "head_ready", "head_taken", "dve_chain") as \
            (block, scores_ready, weighted, sums_ready, head_ready, head_taken, dve_chain):
        ps0 = chip.psum[:, 0:1024].rearrange("p (h t) -> p h t", t=T)
        ps1 = chip.bank(2).rearrange("p (h t) -> p h t", t=P)
        den = chip.psum[:, 3 * BANK:5 * BANK]
        out_at = lambda hd: (0, 5 * BANK)[hd % 2]

        @block.tensor
        def _(pe):
            for hd in range(H_ML):
                for c in range(per_head):
                    m = hd * per_head + c
                    pe.matmul(ps0[:, hd, :], k[:, m, 0:P], q[:, m, :], start=(c == 0), stop=(c == per_head - 1))
                for c in range(per_head):
                    m = hd * per_head + c
                    ins = pe.matmul(ps1[:, hd, :], k[:, m, P:T], q[:, m, P:T], start=(c == 0), stop=(c == per_head - 1))
            ins.then_inc(scores_ready, 1)
            pe.wait_ge(weighted, 1)
            ones = chip.con("ones")
            flat = s0.rearrange("p h t -> p (h t)")
            for n in range(2):
                pe.matmul(den[:, n * BANK:(n + 1) * BANK], ones, flat[:, n * BANK:(n + 1) * BANK],
                          start=True, stop=False, skip_group_check=True)
                for hd in (2 * n, 2 * n + 1):
                    ins = pe.matmul(den[:, hd * T + P:(hd + 1) * T], ones, s1[:, hd, :], start=False,
                                    stop=(hd % 2 == 1), skip_group_check=True)
            ins.then_inc(sums_ready, 1)
            for hd in range(H_ML):
                if hd >= 2:
                    pe.wait_ge(head_taken, hd - 1)
                for c in range(per_head):
                    m = hd * per_head + c
                    out = chip.psum[:, out_at(hd) + c * T:out_at(hd) + (c + 1) * T]
                    pe.matmul(out, v[:, 0, m * P:(m + 1) * P], s0[:, hd, :], start=True, stop=False,
                              skip_group_check=True)
                    ins = pe.matmul(out[:, P:T], v[:, 1, m * P:(m + 1) * P], s1[:, hd, :], start=False, stop=True,
                                    skip_group_check=True)
                ins.then_inc(head_ready, 1)

        @block.vector
        def _(dve):
            chain = Chain(dve, dve_chain)
            dve.wait_ge(scores_ready, 1)
            dve.tensor_tensor(s0, ps0, w0, ALU.mult)
            dve.tensor_tensor(s1, ps1, w1, ALU.mult).then_inc(weighted, 1)
            dve.wait_ge(sums_ready, 1)
            chain(dve.tensor_copy(rden, den))
            chain(dve.scalar_tensor_tensor(rden, rden, -1.0, rden, ALU.mult, ALU.max))
            chain(dve.tensor_tensor(rden, rden, floor.rearrange("p h t -> p (h t)"), ALU.max))
            chain(dve.reciprocal(rden, rden))
            for hd in range(H_ML):
                dve.wait_ge(head_ready, hd + 1)
                ps = chip.psum[:, out_at(hd):out_at(hd) + per_head * T].rearrange("p (c t) -> p c t", t=T)
                dve.tensor_tensor(hc[:, hd * per_head:(hd + 1) * per_head, :], ps,
                                  over(rden[:, hd * T:(hd + 1) * T], per_head), ALU.mult).then_inc(head_taken, 1)

    norm(chip, hc, hc, k, H_ML, per_head, P, LN_EPS, gain=lambda n: chip.col("ml_norm", n), center=True)
    with stage(chip) as (block,):
        @block.vector
        def _(dve):
            for m in range(K_ML):
                dve.scalar_tensor_tensor(hc[:, m, :], xc[:, m, :], chip.col("ml_skip", m), hc[:, m, :],
                                         ALU.mult, ALU.add)
    project(chip, ("ml_z", i), lambda m, k: h[:, k, :], KD,
            silu_into(lambda m: hc[:, m, :], [k[:, n, :] for n in range(2)], times=lambda m: hc[:, m, :]))
    project(chip, ("ml_down", i), lambda m, k: hc[:, k, :], K_ML, residual(chip, i, 0))


def stick_breaking(chip, i):
    h = slot2(chip, 0)
    qk = chip.place(SLOT, 2 * KD, T)
    v = chip.place(3 * SLOT, NT, D)
    o = slot2(chip, 4)
    n0, n1 = 8 * T, 8 * P
    z, sp_, t = (chip.place(5 * SLOT + n * (n0 + n1), n0 + n1) for n in range(3))
    project(chip, ("sb_qk", i), lambda m, k: h[:, k, :], KD, store_with_act(lambda m: qk[:, m, :]))
    project_tokens(chip, ("sb_v", i), lambda k: h[:, k, :], KD, lambda tt, n: v[:, tt, n * BANK:(n + 1) * BANK])
    scale = float(D_SB) ** -0.5
    first = lambda ap: ap[:, 0:n0].rearrange("p (h t) -> p h t", t=T)
    second = lambda ap: ap[:, n0:n0 + n1].rearrange("p (h t) -> p h t", t=P)
    for group in range(2):
        with stage(chip, "scores_ready", "size_ready", "exp_ready", "log_ready", "masked", "sums_ready",
                   "exponents_ready", "weights_ready", "out_ready", "dve_chain") as \
                (block, scores_ready, size_ready, exp_ready, log_ready, masked, sums_ready,
                 exponents_ready, weights_ready, out_ready, dve_chain):
            ps = chip.psum[:, 0:n0 + n1]

            @block.tensor
            def _(pe):
                for odd in range(2):
                    rows = slice(odd * D_SB, (odd + 1) * D_SB)
                    for e in range(4):
                        c, n = 4 * group + e, odd * 4 + e
                        pe.matmul(first(ps)[:, n, :], qk[rows, KD + c, 0:P], qk[rows, c, :], start=True, stop=True)
                        ins = pe.matmul(second(ps)[:, n, :], qk[rows, KD + c, P:T], qk[rows, c, P:T],
                                        start=True, stop=True)
                ins.then_inc(scores_ready, 1)
                pe.wait_ge(masked, 1)
                from_here, ones = chip.con("from_here"), chip.con("ones")
                for n in range(4):
                    sl = slice(n * BANK, (n + 1) * BANK)
                    pe.matmul(ps[:, sl], from_here, sp_[:, sl], start=True, stop=False, skip_group_check=True)
                    for hd in (2 * n, 2 * n + 1):
                        pe.matmul(first(ps)[:, hd, P:T], ones, second(sp_)[:, hd, :], start=False,
                                  stop=(hd % 2 == 1), skip_group_check=True)
                for n in (4, 5):
                    sl = slice(n * BANK, (n + 1) * BANK)
                    ins = pe.matmul(ps[:, sl], from_here, sp_[:, sl], start=True, stop=True)
                ins.then_inc(sums_ready, 1)
                pe.wait_ge(weights_ready, 1)
                for odd in range(2):
                    rows = slice(odd * D_SB, (odd + 1) * D_SB)
                    for e in range(4):
                        n, hd = odd * 4 + e, 2 * (4 * group + e) + odd
                        out = chip.psum[rows, 6 * BANK + e * T:6 * BANK + (e + 1) * T]
                        vh = slice(hd * D_SB, (hd + 1) * D_SB)
                        pe.matmul(out, v[:, 0, vh], first(t)[:, n, :], start=True, stop=False, skip_group_check=True)
                        ins = pe.matmul(out[:, P:T], v[:, 1, vh], second(t)[:, n, :], start=False, stop=True,
                                        skip_group_check=True)
                ins.then_inc(out_ready, 1)

            @block.scalar
            def _(act):
                act.wait_ge(size_ready, 1)
                act.activation(sp_, t, ACT.Exp, scale=-1.0).then_inc(exp_ready, 1)
                act.wait_ge(exp_ready, 1)
                act.activation(sp_, sp_, ACT.Ln, bias=1.0).then_inc(log_ready, 1)
                act.wait_ge(exponents_ready, 1)
                act.activation(t, t, ACT.Exp).then_inc(exp_ready, 1)

            @block.vector
            def _(dve):
                chain = Chain(dve, dve_chain)
                dve.wait_ge(scores_ready, 1)
                chain(dve.tensor_scalar(z, ps, scale, None, ALU.mult))
                dve.scalar_tensor_tensor(t, z, -1.0, z, ALU.mult, ALU.max).then_inc(size_ready, 1)
                dve.wait_ge(log_ready, 1)
                chain(dve.scalar_tensor_tensor(sp_, z, 0.0, sp_, ALU.max, ALU.add))
                masks = ((first, over(chip.con("strict", cols=T), 8)), (second, over(chip.con("strict", cols=P), 8)))
                for part, mask in masks:
                    ins = dve.tensor_tensor(part(sp_), part(sp_), mask, ALU.mult)
                ins.then_inc(masked, 1)
                dve.wait_ge(sums_ready, 1)
                chain(dve.tensor_tensor(t, z, ps, ALU.subtract))
                dve.tensor_scalar(t, t, 0.0, None, ALU.min).then_inc(exponents_ready, 1)
                dve.wait_ge(exp_ready, 2)
                for part, mask in masks:
                    ins = dve.tensor_tensor(part(t), part(t), mask, ALU.mult)
                ins.then_inc(weights_ready, 1)
                dve.wait_ge(out_ready, 1)
                dve.tensor_copy(o[:, 4 * group:4 * group + 4, :],
                                chip.psum[:, 6 * BANK:8 * BANK].rearrange("p (h t) -> p h t", t=T))
    project(chip, ("sb_out", i), lambda m, k: o[:, k, :], KD, residual(chip, i, 0))


MIXERS = (conformer, hgrn, mlstm, stick_breaking)


def second_network(chip):
    for i in LAYERS:
        modulate(chip, i, 0)
        MIXERS[i](chip, i)
        post_norm(chip, i, 0)
        modulate(chip, i, 1)
        conv_ffn(chip, i)
        post_norm(chip, i, 1)


def build(nc, x_in, cols_in, const_in, stream, positions, out, groups, columns, constants, n_units):
    with ExitStack() as ctx:
        chip = Chip(nc, ctx, stream, groups, columns, constants, n_units)
        load_inputs(chip, x_in, cols_in, const_in, positions)
        prepare_conditioning(chip)
        for l in range(L1):
            first_layer(chip, l)
            finish_conditioning(chip, (2 * l, 2 * l + 1))
        second_network(chip)
        with stage(chip) as (block,):
            @block.sync
            def _(sp):
                sp.dma_start(out, chip.x[:, :]).then_inc(chip.out_written, 16)
                sp.wait_ge(chip.out_written, 16)


def features_first(a, rows=P):
    return a.reshape(-1, rows).T


def kernel(**inputs):
    import concourse.bacc as bacc
    from concourse.bass_utils import run_bass_kernel_spmd

    groups = weight_order()
    n_units = place_weights(groups)
    stream = np.zeros((n_units, P, UNIT), np.float32)
    for blocks in groups.values():
        for b in blocks:
            source = np.asarray(inputs[b.array])[b.lead]
            to = stream[b.unit, 0:b.height, b.at:b.at + b.width]
            if b.side:
                for k, c, at, n in b.pieces():
                    to[:, at:at + n] = source[k * P:(k + 1) * P, c:c + n]
            elif b.diagonal:
                for g, small in enumerate(source[b.rows[0]:b.rows[1]]):
                    to[4 * g:4 * g + 4, 4 * g:4 * g + 4] = small
            else:
                rows = source[b.rows[0]:b.rows[1]]
                at = 0
                for c0, c1 in b.cols:
                    to[:, at:at + c1 - c0] = rows[:, c0:c1]
                    at += c1 - c0
    columns = parameter_columns()
    cols = np.zeros((P, columns.n), np.float32)
    for array, index, n, rows, at in columns.parts:
        a = np.asarray(inputs[array])[index]
        if rows is None:
            a = a.reshape(n, P, -1).transpose(1, 0, 2).reshape(P, -1)
            cols[:, at:at + a.shape[1]] = a
        else:
            cols[0:rows, at:at + n] = features_first(a, rows)
    constants, const = shape_constants()
    x = np.asarray(inputs["x"])
    x = np.ascontiguousarray(x[0].reshape(T, KD, P).transpose(2, 1, 0)).reshape(P, KD * T)
    positions = np.ascontiguousarray(inputs["positions"])
    arrays = {"stream": stream, "cols": cols, "const": const, "x": x, "positions": positions}

    nc = bacc.Bacc("TRN2", target_bir_lowering=False, num_devices=1)
    dram = {n: nc.dram_tensor(n + "_dram", a.shape, mybir.dt.from_np(a.dtype), kind="ExternalInput").ap()
            for n, a in arrays.items()}
    out = nc.dram_tensor("out_dram", (P, KD * T), F32, kind="ExternalOutput").ap()
    build(nc, dram["x"], dram["cols"], dram["const"], dram["stream"], dram["positions"], out,
          groups, columns, constants, n_units)
    r = run_bass_kernel_spmd(nc, [{n + "_dram": a for n, a in arrays.items()}], core_ids=[0])
    got = r.results[0]["out_dram"]
    return np.ascontiguousarray(got.reshape(P, KD, T).transpose(2, 1, 0)).reshape(1, T, D)
```
